# Optimizing a Trainium2 kernel written in Bass

```python
import jax, jax.numpy as jnp
from jax import lax
import numpy as np

D_MODEL = 2048
BATCH = 1
SEQ = 256
DEPTH = 2

N_MIXERS = 2
N_MLA_LAYERS = (DEPTH + 1) // 2
N_SB_LAYERS = DEPTH // 2

MLA_HEADS = 16
Q_LORA_RANK = 512
KV_LORA_RANK = 512
QK_NOPE_DIM = 128
QK_ROPE_DIM = 64
V_HEAD_DIM = 128
ROPE_THETA = 10000.0

SB_HEADS = 16
SB_HEAD_DIM = 128

D_FF = ((8 * D_MODEL + 3 * 256 - 1) // (3 * 256)) * 256

Q_BLOCK = 128
RMS_EPS = 1e-6

kernel_name = "hybrid_mla_stickbreaking_trunk"

def _rmsnorm(x, g):
    xf = x.astype(jnp.float32)
    y = xf * lax.rsqrt(jnp.mean(xf * xf, axis=-1, keepdims=True) + RMS_EPS)
    return (y * g.astype(jnp.float32)).astype(x.dtype)

def _rope_tables(positions):
    inv_freq = ROPE_THETA ** (-jnp.arange(0, QK_ROPE_DIM, 2, dtype=jnp.float32) / QK_ROPE_DIM)
    ang = positions.astype(jnp.float32)[..., None] * inv_freq
    return jnp.cos(ang), jnp.sin(ang)

def _apply_rope(x, cos, sin):
    xf = x.astype(jnp.float32)
    x1, x2 = jnp.split(xf, 2, axis=-1)
    out = jnp.concatenate([x1 * cos - x2 * sin, x2 * cos + x1 * sin], axis=-1)
    return out.astype(x.dtype)

def _sweep_query_blocks(block_fn, q_parts):
    b, s = q_parts[0].shape[:2]
    n_blk = s // Q_BLOCK
    blocked = tuple(jnp.moveaxis(q.reshape((b, n_blk, Q_BLOCK) + q.shape[2:]), 1, 0) for q in q_parts)
    out = lax.map(block_fn, blocked + (jnp.arange(n_blk, dtype=jnp.int32),))
    out = jnp.moveaxis(out, 0, 1)
    return out.reshape(b, s, -1)

def _mla_mixer(h, positions, w_in, q_norm, kv_norm, w_uq, w_ukv, w_o):
    b, s, _ = h.shape
    proj = h @ w_in
    c_q = _rmsnorm(proj[..., :Q_LORA_RANK], q_norm)
    c_kv = _rmsnorm(proj[..., Q_LORA_RANK:Q_LORA_RANK + KV_LORA_RANK], kv_norm)
    k_rope = proj[..., Q_LORA_RANK + KV_LORA_RANK:]
    q = (c_q @ w_uq).reshape(b, s, MLA_HEADS, QK_NOPE_DIM + QK_ROPE_DIM)
    q_nope, q_rope = q[..., :QK_NOPE_DIM], q[..., QK_NOPE_DIM:]
    kv = (c_kv @ w_ukv).reshape(b, s, MLA_HEADS, QK_NOPE_DIM + V_HEAD_DIM)
    k_nope, v = kv[..., :QK_NOPE_DIM], kv[..., QK_NOPE_DIM:]
    cos, sin = _rope_tables(positions)
    q_rope = _apply_rope(q_rope, cos[:, :, None, :], sin[:, :, None, :])
    k_rope = _apply_rope(k_rope, cos, sin)
    scale = (QK_NOPE_DIM + QK_ROPE_DIM) ** -0.5
    k_idx = jnp.arange(s, dtype=jnp.int32)

    def block(args):
        qn, qr, blk = args
        q_idx = blk * Q_BLOCK + jnp.arange(Q_BLOCK, dtype=jnp.int32)
        sc = (jnp.einsum('bqhd,bkhd->bhqk', qn, k_nope)
              + jnp.einsum('bqhr,bkr->bhqk', qr, k_rope)).astype(jnp.float32) * scale
        causal = k_idx[None, :] <= q_idx[:, None]
        p = jax.nn.softmax(jnp.where(causal, sc, -jnp.inf), axis=-1)
        return jnp.einsum('bhqk,bkhd->bqhd', p.astype(v.dtype), v)

    o = _sweep_query_blocks(block, (q_nope, q_rope))
    return o @ w_o

def _stick_breaking_mixer(h, w_in, w_o):
    b, s, _ = h.shape
    qkv = (h @ w_in).reshape(b, s, 3, SB_HEADS, SB_HEAD_DIM)
    q, k, v = qkv[:, :, 0], qkv[:, :, 1], qkv[:, :, 2]
    scale = SB_HEAD_DIM ** -0.5
    k_idx = jnp.arange(s, dtype=jnp.int32)

    def block(args):
        qb, blk = args
        q_idx = blk * Q_BLOCK + jnp.arange(Q_BLOCK, dtype=jnp.int32)
        z = jnp.einsum('bqhd,bkhd->bhqk', qb, k).astype(jnp.float32) * scale
        strict = k_idx[None, :] < q_idx[:, None]
        log_beta = jax.nn.log_sigmoid(z)
        log_one_minus = jnp.where(strict, jax.nn.log_sigmoid(-z), 0.0)
        after = lax.cumsum(log_one_minus, axis=log_one_minus.ndim - 1, reverse=True) - log_one_minus
        a = jnp.where(strict, jnp.exp(log_beta + after), 0.0)
        return jnp.einsum('bhqk,bkhd->bqhd', a.astype(v.dtype), v)

    o = _sweep_query_blocks(block, (q,))
    return o @ w_o

def _swiglu(h, w_gate_up, w_down):
    gu = h @ w_gate_up
    g, u = gu[..., :D_FF], gu[..., D_FF:]
    return (jax.nn.silu(g) * u) @ w_down

def setup_inputs(seed: int = 0) -> dict:
    key = jax.random.key(seed)
    ks = jax.random.split(key, 16)

    def dense(k, shape):
        return jax.random.normal(k, shape, jnp.float32) * (shape[-2] ** -0.5)

    def gain(k, shape):
        return 1.0 + 0.02 * jax.random.normal(k, shape, jnp.float32)

    x = jax.random.normal(ks[0], (BATCH, SEQ, D_MODEL), jnp.float32)
    positions = jnp.broadcast_to(jnp.arange(SEQ, dtype=jnp.int32), (BATCH, SEQ))
    return {
        "x": x,
        "positions": positions,
        "attn_norm": gain(ks[1], (DEPTH, D_MODEL)),
        "mla_w_in": dense(ks[2], (N_MLA_LAYERS, D_MODEL, Q_LORA_RANK + KV_LORA_RANK + QK_ROPE_DIM)),
        "mla_q_norm": gain(ks[3], (N_MLA_LAYERS, Q_LORA_RANK)),
        "mla_kv_norm": gain(ks[4], (N_MLA_LAYERS, KV_LORA_RANK)),
        "mla_w_uq": dense(ks[5], (N_MLA_LAYERS, Q_LORA_RANK, MLA_HEADS * (QK_NOPE_DIM + QK_ROPE_DIM))),
        "mla_w_ukv": dense(ks[6], (N_MLA_LAYERS, KV_LORA_RANK, MLA_HEADS * (QK_NOPE_DIM + V_HEAD_DIM))),
        "mla_w_o": dense(ks[7], (N_MLA_LAYERS, MLA_HEADS * V_HEAD_DIM, D_MODEL)),
        "sb_w_in": dense(ks[8], (N_SB_LAYERS, D_MODEL, 3 * SB_HEADS * SB_HEAD_DIM)),
        "sb_w_o": dense(ks[9], (N_SB_LAYERS, SB_HEADS * SB_HEAD_DIM, D_MODEL)),
        "ffn_norm": gain(ks[10], (DEPTH, D_MODEL)),
        "ffn_w_gate_up": dense(ks[11], (DEPTH, D_MODEL, 2 * D_FF)),
        "ffn_w_down": dense(ks[12], (DEPTH, D_FF, D_MODEL)),
        "final_norm": gain(ks[13], (D_MODEL,)),
    }

def reference(x, positions, attn_norm, mla_w_in, mla_q_norm, mla_kv_norm, mla_w_uq, mla_w_ukv,
              mla_w_o, sb_w_in, sb_w_o, ffn_norm, ffn_w_gate_up, ffn_w_down, final_norm):
    h = x
    for i in range(DEPTH):
        a = _rmsnorm(h, attn_norm[i])
        j = i // N_MIXERS
        if i % N_MIXERS == 0:
            mix = _mla_mixer(a, positions, mla_w_in[j], mla_q_norm[j], mla_kv_norm[j],
                             mla_w_uq[j], mla_w_ukv[j], mla_w_o[j])
        else:
            mix = _stick_breaking_mixer(a, sb_w_in[j], sb_w_o[j])
        h = h + mix
        f = _rmsnorm(h, ffn_norm[i])
        h = h + _swiglu(f, ffn_w_gate_up[i], ffn_w_down[i])
    return _rmsnorm(h, final_norm)


_drawn_inputs = setup_inputs


def setup_inputs(seed=0):
    import zlib

    import numpy as np

    out = dict(_drawn_inputs(seed))
    spreads = {}
    factors = {'attn_norm': 3.774,
     'mla_q_norm': 8.0,
     'mla_kv_norm': 8.0,
     'ffn_norm': 2.836,
     'final_norm': 2.764}
    for name, (base, spread) in spreads.items():
        noise = np.random.default_rng([zlib.crc32(name.encode()), seed]).standard_normal(out[name].shape)
        drawn = base * np.exp(spread * noise) if base else spread * noise
        out[name] = __import__('jax').numpy.asarray(drawn.astype(out[name].dtype))
    for name, factor in factors.items():
        out[name] = (out[name] * factor).astype(out[name].dtype)
    return out
```

```python
from contextlib import ExitStack

import numpy as np

import concourse.bass as bass
from concourse import mybir

F32 = mybir.dt.float32
F32R = mybir.dt.float32r
BF16 = mybir.dt.bfloat16
I32 = mybir.dt.int32
ACT = mybir.ActivationFunctionType
ALU = mybir.AluOpType
AX_X = mybir.AxisListType.X

P = 128
M = 2
D = 2048
KD = D // P
LORA = 512
KL = LORA // P
NOPE, ROPE, VD = 128, 64, 128
HEADS, GH = 16, 4
GROUPS = HEADS // GH
FF = 5632
KF = FF // P
CW = 512
PAIRS = FF // CW
HW = 1024
RAW, CUT = 8, 4
LA = 3
EPS = 1e-6
MLA_SCALE = float(NOPE + ROPE) ** -0.5
SB_SCALE = float(128) ** -0.5
MASKED = -1e30
BIG = 3.0e38
THETA = 10000.0


class Body:

    def __init__(self, name, n, iters=1):
        self.name, self.n, self.iters = name, n, iters


class Stream:

    def __init__(self, bodies):
        self.bodies = bodies
        count, fills = 0, [0] * RAW
        last_raw, last_cut = {}, {}
        for b in bodies:
            b.base, b.fills = count, list(fills)
            b.per = [len(range(s, b.n, RAW)) for s in range(RAW)]
            b.raw_gap, b.cut_gap = {}, {}
            for it in range(b.iters):
                for j in range(b.n):
                    r = b.base + it * b.n + j
                    if j % RAW in last_raw:
                        b.raw_gap[j] = min(b.raw_gap.get(j, RAW), r - last_raw[j % RAW])
                    if j % CUT in last_cut:
                        b.cut_gap[j] = min(b.cut_gap.get(j, CUT), r - last_cut[j % CUT])
                    last_raw[j % RAW] = last_cut[j % CUT] = r + 1
            count += b.iters * b.n
            fills = [f + b.iters * q for f, q in zip(fills, b.per)]
        for b, nxt in zip(bodies, bodies[1:]):
            if b.iters > 1:
                for j in range(LA):
                    assert b.base + b.iters * b.n == nxt.base and b.fills[j] + b.iters * b.per[j] == nxt.fills[j]
                    b.cut_gap[j] = min(b.cut_gap[j], nxt.cut_gap[j])

    def ahead(self, b, it, j):
        if j + LA < b.n:
            return b, it, j + LA
        if b.iters > 1:
            return b, it + 1, j + LA - b.n
        k = self.bodies.index(b) + 1
        return (self.bodies[k], 0, j + LA - b.n) if k < len(self.bodies) else None

    def number(self, b, it, j):
        return it * b.n + (b.base + j)

    def landed(self, b, it, j):
        return it * (16 * b.per[j % RAW]) + 16 * (b.fills[j % RAW] + j // RAW + 1)


def trunk(nc, x, positions, attn_norm, mla_w_in, mla_q_norm, mla_kv_norm, mla_w_uq, mla_w_ukv,
          mla_w_o, sb_w_in, sb_w_o, ffn_norm, ffn_w_gate_up, ffn_w_down, final_norm, inv_freq, out):
    bodies = {
        "win": Body("win", 17),
        "mla0": Body("mla0", 7), "mla": Body("mla", 7, GROUPS - 1),
        "wo0a": Body("wo0a", 16), "wo0b": Body("wo0b", 16),
        "gu0a": Body("gu0a", 16), "gu0": Body("gu0", 16, PAIRS - 1), "down0": Body("down0", 44, 2),
        "sb0": Body("sb0", 24), "sb": Body("sb", 24, GROUPS - 1),
        "wo1a": Body("wo1a", 16), "wo1b": Body("wo1b", 16),
        "gu1a": Body("gu1a", 16), "gu1": Body("gu1", 16, PAIRS - 1),
        "down1a": Body("down1a", 44), "down1b": Body("down1b", 44),
    }
    st = Stream(list(bodies.values()))

    def rows(w, k, n, c0, cols):
        return w[k * P:(k + n) * P, bass.ds(c0, cols)].rearrange("(t p) c -> p t c", p=P)

    w_in, w_uq, w_ukv = mla_w_in[0], mla_w_uq[0], mla_w_ukv[0]
    HQ = GH * (NOPE + ROPE)
    HKV = GH * (NOPE + VD)

    def src_win(it, j):
        return rows(w_in, 2 * (j % 8), 2, CW * (j // 8), CW) if j < 16 else rows(w_in, 0, KD, 2 * LORA, ROPE)

    def src_mla(g):
        def src(it, j):
            if j < 3:
                return rows(w_uq, 0, KL, (it + g) * HQ + 256 * j, 256)
            return rows(w_ukv, 2 * ((j - 3) % 2), 2, (it + g) * HKV + CW * ((j - 3) // 2), CW)
        return src

    def src_wo(w, n):
        return lambda it, j: rows(w, 2 * (j % 8), 2, CW * (n + j // 8), CW)

    def src_gu(w, c):
        return lambda it, j: rows(w, 2 * (j % 8), 2, (it + c) * CW + FF * (j // 8), CW)

    def src_down(w, c):
        return lambda it, j: rows(w, 2 * (j % 22), 2, (2 * it + c + j // 22) * CW, CW)

    def src_sb(g):
        return lambda it, j: rows(sb_w_in[0], 2 * (j % 8), 2, (it + g) * CW + D * (j // 8), CW)

    source = {
        "win": src_win, "mla0": src_mla(0), "mla": src_mla(1),
        "wo0a": src_wo(mla_w_o[0], 0), "wo0b": src_wo(mla_w_o[0], 2),
        "gu0a": src_gu(ffn_w_gate_up[0], 0), "gu0": src_gu(ffn_w_gate_up[0], 1),
        "down0": src_down(ffn_w_down[0], 0),
        "sb0": src_sb(0), "sb": src_sb(1),
        "wo1a": src_wo(sb_w_o[0], 0), "wo1b": src_wo(sb_w_o[0], 2),
        "gu1a": src_gu(ffn_w_gate_up[1], 0), "gu1": src_gu(ffn_w_gate_up[1], 1),
        "down1a": src_down(ffn_w_down[1], 0), "down1b": src_down(ffn_w_down[1], 2),
    }

    with ExitStack() as ctx:
        top = [nc.sbuf_base]

        def at(name, shape, dt, offset):
            return nc.alloc_sbuf_tensor_at(name, shape, dt, offset=offset)

        def size(shape, dt):
            return int(np.prod(shape[1:])) * (2 if dt == BF16 else 4)

        def sb(name, shape, dt):
            off = (top[0] + 63) // 64 * 64
            top[0] = off + size(shape, dt)
            return at(name, shape, dt, off)

        def sem(name):
            return ctx.enter_context(nc.semaphore(name))

        h = sb("h", [P, M, D], F32)
        xt_hi = sb("xt_hi", [P, KD, M * P], F32R)
        xt_lo = sb("xt_lo", [P, KD, M * P], F32R)
        gfin = at("gfin", [P, D], F32, top[0] - size([P, KD, M * P], F32R))
        w_raw = sb("w_raw", [P, RAW, HW], F32)
        w_hi = sb("w_hi", [P, CUT, HW], F32R)
        w_lo = sb("w_lo", [P, CUT, HW], F32R)
        area = (top[0] + 63) // 64 * 64
        hid_hi = sb("hid_hi", [P, KF, M * P], F32R)
        hid_lo = sb("hid_lo", [P, KF, M * P], F32R)
        area_end, area_top = top[0], [area]

        def part(name, shape, dt):
            off = area_top[0]
            area_top[0] += size(shape, dt)
            assert area_top[0] <= area_end
            return at(name, shape, dt, off)

        ot_hi = part("ot_hi", [P, HEADS, M * P], F32R)
        ot_lo = part("ot_lo", [P, HEADS, M * P], F32R)
        qkt = part("qkt", [P, GH, 2, M * P], F32)
        pb = part("pb", [P, 2, 3 * P], F32)
        pt = part("pt", [P, 2, 3 * P], F32)
        mixer_top = area_top[0]
        ct_hi = part("ct_hi", [P, 2 * KL, M * P], F32R)
        ct_lo = part("ct_lo", [P, 2 * KL, M * P], F32R)
        qg = part("qg", [P, M, GH, NOPE + ROPE], F32)
        qrg = part("qrg", [P, M, GH, ROPE], F32)
        kvg = part("kvg", [P, M, GH, NOPE + VD], F32)
        qrt = part("qrt", [P, 2, M * P], F32)
        area_top[0] = mixer_top
        sq = part("sq", [P, M, CW], F32)
        sk = part("sk", [P, M, CW], F32)
        sv = part("sv", [P, M, CW], F32)
        sabs = part("sabs", [P, 2, 3 * P], F32)
        sexp = part("sexp", [P, 2, 3 * P], F32)
        sln = part("sln", [P, 2, 3 * P], F32)
        ssp = part("ssp", [P, 2, 3 * P], F32)

        sg = sb("sg", [P, M, CW], F32)
        hm = sb("hm", [P, M, CW], F32)
        junk = [t_[:, :, :].rearrange("p m c -> p (m c)").bitcast(BF16) for t_ in (sg, hm)]
        ident = sb("ident", [P, P], F32)
        ident_h = sb("ident_h", [P, P], BF16)
        causal = sb("causal", [P, P], BF16)
        strict = sb("strict", [P, P], F32)
        neg_tri = sb("neg_tri", [P, P], F32)
        neg_one = sb("neg_one", [P, P], F32)
        NG = 4 * KD + 2 * KL
        gain_rows = sb("gain_rows", [NG, P], F32)
        gain = sb("gain", [P, NG], F32)
        pos_i = sb("pos_i", [P, M], I32)
        pos_f = sb("pos_f", [P, M], F32)
        inv_f = sb("inv_f", [P, ROPE // 2], F32)
        ang = sb("ang", [P, M, ROPE // 2], F32)
        turns = sb("turns", [P, M, ROPE // 2], F32)
        red_s = sb("red_s", [P, M, ROPE // 2], F32)
        red_c = sb("red_c", [P, M, ROPE // 2], F32)
        rope_c = sb("rope_c", [P, M, ROPE], F32)
        rope_s = sb("rope_s", [P, M, ROPE], F32)
        r_t1 = sb("r_t1", [P, M, GH, ROPE], F32)
        r_t2 = sb("r_t2", [P, M, GH, ROPE], F32)
        kr = sb("kr", [P, M, ROPE], F32)
        kr_pad = sb("kr_pad", [P, 2, M, P], F32)
        krt = sb("krt", [P, 2, M * P], F32)
        ssq = sb("ssq", [P, M], F32)
        ms = sb("ms", [P, M], F32)
        ln_ms = sb("ln_ms", [P, M], F32)
        y0 = sb("y0", [P, M], F32)
        nt = sb("nt", [P, M], F32)
        rstd = sb("rstd", [P, M], F32)
        rstd_q = sb("rstd_q", [P, M], F32)
        rstd_kv = sb("rstd_kv", [P, M], F32)
        nmax = sb("nmax", [P, 2, M], F32)
        nmax_s = sb("nmax_s", [P, 2, M], F32)
        psums = sb("psums", [P, 2, M], F32)
        prec = sb("prec", [P, 2, M], F32)
        assert top[0] <= nc.sbuf_usable_end, (top[0], nc.sbuf_usable_end)

        def bank(name, shape):
            return ctx.enter_context(nc.psum_tensor(name, shape, F32))

        acc = [[bank(f"acc{a}{m}", [P, CW]) for m in range(M)] for a in range(2)]
        tp = [bank(f"tp{b}", [P, CW]) for b in range(2)]
        sc = bank("sc", [P, CW])
        pv = bank("pv", [P, CW])
        zb = [sc, tp[1]]

        landed = [sem(f"w_landed{s}") for s in range(RAW)]
        hi_done = sem("w_hi_done")
        lo_done = sem("w_lo_done")
        half_used = sem("w_half_used")
        x_landed = sem("x_landed")
        small_landed = sem("small_landed")
        gfin_landed = sem("gfin_landed")
        consts_done = sem("consts_done")
        pool_step = sem("pool_step")
        gain_full = sem("gain_full")
        gain_done = sem("gain_done")
        acc_free = [[sem(f"acc{a}{m}_free") for m in range(M)] for a in range(2)]
        tp_full = [sem(f"tp{b}_full") for b in range(2)]
        tp_free = [sem(f"tp{b}_free") for b in range(2)]
        t_hi_done = sem("t_hi_done")
        ssq_done = sem("ssq_done")
        ms_done = sem("ms_done")
        ln_done = sem("ln_done")
        y0_done = sem("y0_done")
        rstd_done = sem("rstd_done")
        dve_step = sem("dve_step")
        rope_ready = sem("rope_ready")
        angles_done = sem("angles_done")
        sin_done = sem("sin_done")
        pos_landed = sem("pos_landed")
        kr_step = sem("kr_step")
        kr_done = sem("kr_done")
        q_step = sem("q_rope_step")
        sb_scale_done = sem("sb_scale_done")
        nmax_done = sem("nmax_done")
        prec_done = sem("prec_done")
        ssp_step = sem("ssp_step")
        out_ready = sem("out_ready")
        q_rope = sem("q_rope_done")
        sc_full = sem("scores_full")
        max_done = sem("max_done")
        exp_done = sem("exp_done")
        p_done = sem("p_normalised")
        pv_full = sem("pv_full")
        o_hi_done = sem("o_hi_done")
        pv_free = sem("pv_free")
        z_full = sem("z_full")
        abs_done = sem("abs_done")
        sexp_done = sem("sexp_done")
        sln_done = sem("softplus_ln_done")
        ssp_done = sem("softplus_done")
        logw_full = sem("log_weights_full")
        a_exp_done = sem("a_exp_done")
        a_done = sem("a_masked")
        out_stored = sem("out_stored")

        G_ATTN, G_FFN, G_Q, G_KV = (0, KD), (2 * KD, 3 * KD), 4 * KD, 4 * KD + KL

        block = ctx.enter_context(nc.Block())

        @block.sync
        def _(sp):
            x_v = x[0].rearrange("(m p) d -> p m d", p=P)
            for m in range(M):
                sp.dma_start(h[:, m, :], x_v[:, m, :]).then_inc(x_landed, 16)

            def load(b, it):
                for j in range(b.n):
                    s = j % RAW
                    if j in b.raw_gap:
                        sp.wait_ge(lo_done, st.number(b, it, j) - b.raw_gap[j])
                    src = source[b.name](it, j)
                    dst = w_raw[:, s, :].rearrange("p (t c) -> p t c", t=src.shape[1])
                    sp.dma_start(dst, src).then_inc(landed[s], 16)

            for b in st.bodies:
                if b.iters == 1:
                    load(b, 0)
                else:
                    with sp.Fori(0, b.iters) as it:
                        load(b, it)
            sp.wait_ge(half_used, st.number(bodies["down1a"], 0, 0) + 1)
            sp.dma_start(gfin[:, :], final_norm.partition_broadcast(P)).then_inc(gfin_landed, 16)

        @block.gpsimd
        def _(pool):
            pool.memset(ident[:, :], 0.0).then_inc(pool_step, 1)
            pool.memset(ident_h[:, :], 0.0).then_inc(pool_step, 1)
            pool.memset(causal[:, :], 0.0).then_inc(pool_step, 1)
            pool.memset(strict[:, :], 1.0).then_inc(pool_step, 1)
            pool.memset(neg_tri[:, :], -1.0).then_inc(pool_step, 1)
            pool.memset(neg_one[:, :], -1.0).then_inc(consts_done, 1)
            pool.memset(kr_pad[:, :, :, :], 0.0).then_inc(consts_done, 1)
            pool.wait_ge(pool_step, 5)
            for m in (ident, ident_h):
                pool.affine_select(out=m[:, :], in_=m[:, :], compare_op=ALU.not_equal, fill=1.0, base=0,
                                   pattern=[[-1, P]], channel_multiplier=1).then_inc(consts_done, 1)
            pool.affine_select(out=causal[:, :], in_=causal[:, :], compare_op=ALU.is_ge, fill=MASKED,
                               base=0, pattern=[[-1, P]], channel_multiplier=1).then_inc(consts_done, 1)
            pool.affine_select(out=strict[:, :], in_=strict[:, :], compare_op=ALU.is_gt, fill=0.0,
                               base=0, pattern=[[1, P]], channel_multiplier=-1).then_inc(consts_done, 1)
            pool.affine_select(out=neg_tri[:, :], in_=neg_tri[:, :], compare_op=ALU.is_ge, fill=0.0,
                               base=0, pattern=[[-1, P]], channel_multiplier=1).then_inc(consts_done, 1)
        CONSTS, SMALL = 7, 4

        ACC0 = {"win": 0, "mla": 2}
        ACC1 = {"win": 0, "mla": 1}
        ACC0["wo0"], ACC1["wo0"] = ACC0["mla"] + 2 * GROUPS, ACC1["mla"] + 2 * GROUPS
        ACC0["gu0"], ACC1["gu0"] = ACC0["wo0"] + 2, ACC1["wo0"] + 2
        ACC0["down0"], ACC1["down0"] = ACC0["gu0"] + PAIRS, ACC1["gu0"] + PAIRS
        ACC0["sb"], ACC1["sb"] = ACC0["down0"] + 2, ACC1["down0"] + 2
        ACC0["wo1"], ACC1["wo1"] = ACC0["sb"] + 2 * GROUPS, ACC1["sb"] + GROUPS
        ACC0["gu1"], ACC1["gu1"] = ACC0["wo1"] + 2, ACC1["wo1"] + 2
        ACC0["down1"], ACC1["down1"] = ACC0["gu1"] + PAIRS, ACC1["gu1"] + PAIRS
        ACC0["end"], ACC1["end"] = ACC0["down1"] + 2, ACC1["down1"] + 2
        UH = KD // 4
        TP0 = {"win": 0, "lat": UH, "mla": UH + 3}
        TP1 = {"win": 0, "lat": UH, "mla": UH + 2}
        TP0["gu0"], TP1["gu0"] = TP0["mla"] + 5 * GROUPS, TP1["mla"] + 4 * GROUPS
        TP0["pair0"], TP1["pair0"] = TP0["gu0"] + UH, TP1["gu0"] + UH
        TP0["sb"], TP1["sb"] = TP0["pair0"] + PAIRS, TP1["pair0"] + PAIRS
        TP0["sba"], TP1["sba"] = TP0["sb"] + UH, TP1["sb"] + UH
        TP0["gu1"], TP1["gu1"] = TP0["sba"] + GH * GROUPS, TP1["sba"]
        TP0["pair1"], TP1["pair1"] = TP0["gu1"] + UH, TP1["gu1"] + UH
        THI = {"win": 0, "lat": 2 * UH, "gu0": 2 * UH + 4}
        THI["pair0"] = THI["gu0"] + 2 * UH
        THI["sb"] = THI["pair0"] + 2 * PAIRS
        THI["gu1"] = THI["sb"] + 2 * UH
        THI["pair1"] = THI["gu1"] + 2 * UH
        N_ATTN0, N_Q, N_KV, N_FFN0, N_ATTN1, N_FFN1, N_FINAL = range(7)

        @block.tensor
        def _(pe):
            def products(b, it, j, a, hi, lo, k0, nk, n, c0=0, first=False, last=False, free=None):
                if free is not None and not (isinstance(free, int) and free == 0):
                    for m in range(M):
                        pe.wait_ge(acc_free[a][m], free)
                pe.wait_ge(lo_done, st.number(b, it, j) + 1)
                wh = w_hi[:, j % CUT, :].rearrange("p (t c) -> p t c", t=nk)
                wl = w_lo[:, j % CUT, :].rearrange("p (t c) -> p t c", t=nk)
                for k in range(nk):
                    for m in range(M):
                        o = acc[a][m][:, c0:c0 + n]
                        xh = hi[:, k0 + k, m * P:(m + 1) * P]
                        xl = lo[:, k0 + k, m * P:(m + 1) * P]
                        pe.matmul(o, xh, wh[:, k, :], start=first and k == 0, stop=False)
                        pe.matmul(o, xh, wl[:, k, :], start=False, stop=False)
                        mm = pe.matmul(o, xl, wh[:, k, :], start=False, stop=last and k == nk - 1)
                mm.then_inc(half_used, 1)

            def turn(b, before, tiles):
                if not (isinstance(before, int) and before == 0):
                    pe.wait_ge(tp_free[b], before)
                for n, tile in enumerate(tiles):
                    mm = pe.transpose(tp[b][:, n * P:(n + 1) * P], tile, ident[:, :])
                mm.then_inc(tp_full[b], 1)

            def tiles_of(src, k):
                return [src[:, m, kk * P:(kk + 1) * P] for kk in (k, k + 1) for m in range(M)]

            def turn_h(phase, u):
                turn(u % 2, (TP0, TP1)[u % 2][phase] + u // 2, tiles_of(h, 2 * u))

            def turned_h(phase, u):
                pe.wait_ge(tp_free[u % 2], (TP0, TP1)[u % 2][phase] + u // 2 + 1)

            def first_chunk(phase, b, free):
                turn_h(phase, 0)
                turn_h(phase, 1)
                for j in range(8):
                    turned_h(phase, j)
                    products(b, 0, j, 0, xt_hi, xt_lo, 2 * j, 2, CW, first=j == 0, last=j == 7,
                             free=free if j == 0 else None)
                    if j + 2 < 8:
                        turn_h(phase, j + 2)

            def mla_scores(g, x_, v0, v1):
                pe.wait_ge(tp_free[(x_ + 1) % 2], (v1, v0)[x_ % 2] + (1, 2, 2, 3)[x_])
                if x_:
                    pe.wait_ge(exp_done, GH * g + x_)
                for m in range(M):
                    o, keys = sc[:, m * P:], (m + 1) * P
                    q = qkt[:, x_, 0, m * P:(m + 1) * P]
                    qr = qrt[:, x_ // 2, m * P:(m + 1) * P]
                    k_ = qkt[:, x_, 1, :]
                    kr_ = krt[:, x_ % 2, :]
                    pe.matmul(o[:, 0:keys], q, k_[:, 0:keys], start=True, stop=False, skip_group_check=True)
                    pe.matmul(o[:, 0:keys], qr, kr_[:, 0:keys], start=False, stop=False,
                              skip_group_check=True)
                    mm = pe.matmul(o[:, m * P:keys], ident_h[:, :], causal[:, :], start=False, stop=True,
                                   skip_group_check=True)
                mm.then_inc(sc_full, 1)

            def mla_turn_p(g, x_, v0, v1):
                pe.wait_ge(p_done, GH * g + x_ + 1)
                turn((x_ + 1) % 2, (v1, v0)[x_ % 2] + (2, 3, 3, 4)[x_],
                     [pb[:, x_ % 2, n * P:(n + 1) * P] for n in range(3)])

            def weighted(head, x_, v0_, v1_, w):
                if x_:
                    pe.wait_ge(pv_free, head)
                pe.matmul(pv[:, 0:2 * P], v0_, w[:, 0:2 * P], start=True, stop=False)
                pe.matmul(pv[:, P:2 * P], v1_, w[:, 2 * P:3 * P], start=False, stop=True)\
                  .then_inc(pv_full, 1)

            def mla_out(g, x_, v0, v1):
                pe.wait_ge(tp_free[(x_ + 1) % 2], (v1, v0)[x_ % 2] + (3, 4, 4, 5)[x_])
                weighted(GH * g + x_, x_, kvg[:, 0, x_, NOPE:], kvg[:, 1, x_, NOPE:], pt[:, x_ % 2, :])

            def mla_attention(g, j):
                v0, v1 = g * 5 + TP0["mla"], g * 4 + TP1["mla"]

                def q_k(x_):
                    turn((x_ + 1) % 2, (v1, v0)[x_ % 2] + (0, 1, 1, 2)[x_],
                         [qg[:, m, x_, 0:NOPE] for m in range(M)] + [kvg[:, m, x_, 0:NOPE] for m in range(M)])

                if j == 0:
                    pe.wait_ge(q_rope, g * 2 + 2)
                    for m in range(M):
                        pe.wait_ge(acc_free[0][m], g * 2 + ACC0["mla"] + 2)
                        pe.wait_ge(acc_free[1][m], g * 2 + ACC1["mla"] + 2)
                    turn(0, v0, [qrg[:, m, 2 * pr:2 * pr + 2, :].rearrange("p h c -> p (h c)")
                                 for pr in range(2) for m in range(M)])
                    q_k(0)
                elif j == 1:
                    q_k(1)
                    q_k(2)
                    mla_scores(g, 0, v0, v1)
                elif j == 2:
                    q_k(3)
                    mla_scores(g, 1, v0, v1)
                    mla_turn_p(g, 0, v0, v1)
                elif j == 3:
                    mla_scores(g, 2, v0, v1)
                    mla_turn_p(g, 1, v0, v1)
                    mla_out(g, 0, v0, v1)
                elif j == 4:
                    mla_scores(g, 3, v0, v1)
                    mla_turn_p(g, 2, v0, v1)
                    mla_out(g, 1, v0, v1)
                elif j == 5:
                    mla_turn_p(g, 3, v0, v1)
                    mla_out(g, 2, v0, v1)
                elif j == 6:
                    mla_out(g, 3, v0, v1)

            def mla_group(b, it, g, before):
                a0, a1 = g * 2 + ACC0["mla"], g * 2 + ACC1["mla"]
                for j in range(3):
                    products(b, it, j, j // 2, ct_hi, ct_lo, 0, KL, 256, c0=256 * (j % 2), first=True,
                             last=True, free=(a0, None, a1)[j])
                    before(j)
                for j in range(3, 7):
                    a, k = (j - 3) // 2, (j - 3) % 2
                    if isinstance(g, int) and g == 0 and j == 3:
                        pe.wait_ge(tp_free[0], TP0["lat"] + 2)
                        pe.wait_ge(tp_free[1], TP1["lat"] + 2)
                    products(b, it, j, a, ct_hi, ct_lo, KL + 2 * k, 2, CW, first=k == 0, last=k == 1,
                             free=(a0 + 1, a1 + 1)[a] if k == 0 else None)
                    before(j)

            def project_out(b, phase, attention, heads0):
                for j in range(16):
                    if attention:
                        if j < 8:
                            pe.wait_ge(pv_free, heads0 + 2 * j + 2)
                    products(b, 0, j, j // 8, ot_hi, ot_lo, 2 * (j % 8), 2, CW, first=j % 8 == 0,
                             last=j % 8 == 7,
                             free=(ACC0, ACC1)[j // 8][phase] + (0 if attention else 1) if j % 8 == 0 else None)
                    if attention:
                        attention(j)

            def gate_up(layer, b, it, c):
                gu, pr = f"gu{layer}", f"pair{layer}"
                for j in range(16):
                    products(b, it, j, j // 8, xt_hi, xt_lo, 2 * (j % 8), 2, CW, first=j % 8 == 0,
                             last=j % 8 == 7, free=c + (ACC0, ACC1)[j // 8][gu] if j % 8 == 0 else None)
                    if j == 1:
                        turn_pair(layer, c - 1, 0)
                    if j == 2:
                        turn_pair(layer, c - 1, 1)

            def turn_pair(layer, c, u):
                if u == 0:
                    for m in range(M):
                        pe.wait_ge(acc_free[1][m], c + (ACC1[f"gu{layer}"] + 1))
                turn(u, c + (TP0, TP1)[u][f"pair{layer}"], tiles_of(hm, 2 * u))

            def ffn(layer):
                first, loop = bodies[f"gu{layer}a"], bodies[f"gu{layer}"]
                gu = f"gu{layer}"
                for m in range(M):
                    pe.wait_ge(acc_free[0][m], ACC0[gu])
                    pe.wait_ge(acc_free[1][m], ACC1[gu])
                first_chunk(gu, first, ACC0[gu])
                for j in range(8, 16):
                    products(first, 0, j, 1, xt_hi, xt_lo, 2 * (j % 8), 2, CW, first=j == 8, last=j == 15,
                             free=ACC1[gu] if j == 8 else None)
                with pe.Fori(0, PAIRS - 1) as it:
                    gate_up(layer, loop, it, it + 1)
                turn_pair(layer, PAIRS - 1, 0)
                turn_pair(layer, PAIRS - 1, 1)
                down = bodies["down0" if layer == 0 else "down1a"]
                dn = f"down{layer}"
                with pe.Fori(0, 2) as it:
                    for j in range(44):
                        a, k = j // 22, j % 22
                        if k == 20:
                            pe.wait_ge(tp_free[0], TP0[f"pair{layer}"] + PAIRS)
                            pe.wait_ge(tp_free[1], TP1[f"pair{layer}"] + PAIRS)
                        products(down, it, j, a, hid_hi, hid_lo, 2 * k, 2, CW, first=k == 0, last=k == 21,
                                 free=it + (ACC0, ACC1)[a][dn] if k == 0 else None)

            def sb_attention(g, j):
                def head(x_):
                    return g * GH + x_
                if j == 0:
                    for m in range(M):
                        pe.wait_ge(acc_free[0][m], g * 2 + ACC0["sb"] + 2)
                        pe.wait_ge(acc_free[1][m], g + ACC1["sb"] + 1)
                if j < 4:
                    turn(0, g * GH + TP0["sba"] + j,
                         [s[:, m, j * P:(j + 1) * P] for s in (sq, sk) for m in range(M)])
                x_ = j - 1
                if 0 <= x_ < GH:
                    pe.wait_ge(tp_free[0], g * GH + TP0["sba"] + x_ + 1)
                    if x_ >= 2:
                        pe.wait_ge(a_exp_done, head(x_ - 1))
                    z = zb[x_ % 2]
                    pe.matmul(z[:, 0:2 * P], qkt[:, x_, 1, 0:P], qkt[:, x_, 0, :], start=True, stop=False,
                              skip_group_check=True)
                    pe.matmul(z[:, 2 * P:3 * P], qkt[:, x_, 1, P:2 * P], qkt[:, x_, 0, P:2 * P],
                              start=False, stop=False, skip_group_check=True).then_inc(z_full, 1)
                x_ = j - 3
                if 0 <= x_ < GH:
                    pe.wait_ge(a_done, head(x_) + 1)
                    weighted(g * GH + (HEADS + x_), x_, sv[:, 0, x_ * P:(x_ + 1) * P],
                             sv[:, 1, x_ * P:(x_ + 1) * P], pt[:, x_ % 2, :])
                x_ = j - 2
                if 0 <= x_ < GH:
                    pe.wait_ge(ssp_done, head(x_) + 1)
                    z, s_ = zb[x_ % 2], ssp[:, x_ % 2, :]
                    pe.matmul(z[:, 0:2 * P], neg_tri[:, :], s_[:, 0:2 * P], start=False, stop=False,
                              skip_group_check=True)
                    pe.matmul(z[:, P:2 * P], neg_one[:, :], s_[:, 2 * P:3 * P], start=False, stop=False,
                              skip_group_check=True)
                    pe.matmul(z[:, 2 * P:3 * P], neg_tri[:, :], s_[:, 2 * P:3 * P], start=False, stop=True,
                              skip_group_check=True).then_inc(logw_full, 1)

            def sb_group(b, it, g, attention):
                a0, a1 = g * 2 + ACC0["sb"], g + ACC1["sb"]
                for j in range(24):
                    c = j // 8
                    products(b, it, j, c % 2, xt_hi, xt_lo, 2 * (j % 8), 2, CW, first=j % 8 == 0,
                             last=j % 8 == 7, free=(a0, a1, a0 + 1)[c] if j % 8 == 0 else None)
                    attention(j)

            pe.wait_ge(consts_done, CONSTS)
            pe.wait_ge(small_landed, 16 * SMALL)
            pe.transpose(sc[:, 0:NG], gain_rows[:, :], ident[0:NG, 0:NG]).then_inc(gain_full, 1)
            pe.wait_ge(x_landed, 16 * M)

            b = bodies["win"]
            first_chunk("win", b, 0)
            for j in range(8, 16):
                products(b, 0, j, 1, xt_hi, xt_lo, 2 * (j % 8), 2, CW, first=j == 8, last=j == 15)
                if j == 9:
                    for m in range(M):
                        pe.wait_ge(acc_free[0][m], 1)
                    turn(0, TP0["lat"], tiles_of(sg, 0))
                    turn(1, TP1["lat"], tiles_of(sg, 2))
            products(b, 0, 16, 0, xt_hi, xt_lo, 0, KD, ROPE, first=True, last=True, free=1)

            def latents_and_kr(j):
                if j == 0:
                    for m in range(M):
                        pe.wait_ge(acc_free[1][m], 1)
                    turn(0, TP0["lat"] + 1, tiles_of(hm, 0))
                    turn(1, TP1["lat"] + 1, tiles_of(hm, 2))
                if j == 1:
                    pe.wait_ge(kr_done, M * 2)
                    turn(0, TP0["lat"] + 2, [kr_pad[:, a, m, :] for a in range(2) for m in range(M)])

            pe.wait_ge(tp_free[0], TP0["lat"] + 1)
            pe.wait_ge(tp_free[1], TP1["lat"] + 1)
            mla_group(bodies["mla0"], 0, 0, latents_and_kr)
            with pe.Fori(0, GROUPS - 1) as it:
                mla_group(bodies["mla"], it, it + 1, lambda j: mla_attention(it, j))
            project_out(bodies["wo0a"], "wo0", lambda j: mla_attention(GROUPS - 1, j), 0)
            project_out(bodies["wo0b"], "wo0", None, 0)
            ffn(0)

            for m in range(M):
                pe.wait_ge(acc_free[0][m], ACC0["sb"])
                pe.wait_ge(acc_free[1][m], ACC1["sb"])
            b = bodies["sb0"]
            first_chunk("sb", b, ACC0["sb"])
            for j in range(8, 24):
                c = j // 8
                products(b, 0, j, c % 2, xt_hi, xt_lo, 2 * (j % 8), 2, CW, first=j % 8 == 0,
                         last=j % 8 == 7, free=(0, ACC1["sb"], ACC0["sb"] + 1)[c] if j % 8 == 0 else None)
            with pe.Fori(0, GROUPS - 1) as it:
                sb_group(bodies["sb"], it, it + 1, lambda j: sb_attention(it, j))
            project_out(bodies["wo1a"], "wo1", lambda j: sb_attention(GROUPS - 1, j), HEADS)
            project_out(bodies["wo1b"], "wo1", None, HEADS)
            ffn(1)

        @block.scalar
        def _(act):
            def cut(target):
                if target is None:
                    return
                b, it, j = target
                act.wait_ge(landed[j % RAW], st.landed(b, it, j))
                if j in b.cut_gap:
                    act.wait_ge(half_used, st.number(b, it, j) - b.cut_gap[j])
                act.activation(w_hi[:, j % CUT, :], w_raw[:, j % RAW, :], ACT.Copy).then_inc(hi_done, 1)

            def run(name, side):
                b = bodies[name]
                if b.iters == 1:
                    for j in range(b.n):
                        cut(st.ahead(b, 0, j))
                        side(b, 0, j)
                else:
                    with act.Fori(0, b.iters) as it:
                        for j in range(b.n):
                            cut(st.ahead(b, it, j))
                            side(b, it, j)

            def chunk_full(b, it, j):
                act.wait_ge(half_used, st.number(b, it, j) + 1)

            def turned_hi(u, count, thi, dst, gains):
                act.wait_ge(tp_full[u], count)
                if gains is None:
                    act.activation(dst, tp[u][:, :].rearrange("p (t c) -> p t c", t=2), ACT.Copy)\
                       .then_inc(t_hi_done, 1)
                else:
                    act.activation(dst[:, 0, :], tp[u][:, 0:M * P], ACT.Copy, scale=gain[:, gains:gains + 1])
                    act.activation(dst[:, 1, :], tp[u][:, M * P:], ACT.Copy,
                                   scale=gain[:, gains + 1:gains + 2]).then_inc(t_hi_done, 1)

            def turned_h(phase, u, g0):
                turned_hi(u % 2, (TP0, TP1)[u % 2][phase] + u // 2 + 1, None,
                          xt_hi[:, 2 * u:2 * u + 2, :], g0 + 2 * u)

            def squares(norm, src, scratch):
                for m in range(M):
                    act.activation(scratch[m], src[:, m, :], ACT.Square, accum_out=ssq[:, m:m + 1])\
                       .then_inc(ssq_done, 1)

            def root(norm):
                act.wait_ge(ms_done, norm + 1)
                if norm:
                    act.wait_ge(rstd_done, norm)
                act.activation(ln_ms[:, :], ms[:, :], ACT.Ln).then_inc(ln_done, 1)
                act.wait_ge(ln_done, norm + 1)
                act.activation(y0[:, :], ln_ms[:, :], ACT.Exp, scale=-0.5).then_inc(y0_done, 1)

            def phase_start(phase, norm, g0, j):
                if j + 2 < 8:
                    turned_h(phase, j + 2, g0)
                if j == 2:
                    squares(norm, h, junk)
                if j == 3:
                    root(norm)

            with nc.allow_non_contiguous_dma(reason="256 positions, once"):
                act.dma_start(pos_i[:, :], positions.rearrange("b (m p) -> p (b m)", p=P))\
                   .then_inc(pos_landed, 16)
            act.dma_start(inv_f[:, :], inv_freq.partition_broadcast(P)).then_inc(pos_landed, 16)
            act.dma_start(gain_rows[0:2 * KD, :], attn_norm.rearrange("l (k p) -> (l k) p", p=P))\
               .then_inc(small_landed, 16)
            act.dma_start(gain_rows[2 * KD:4 * KD, :], ffn_norm.rearrange("l (k p) -> (l k) p", p=P))\
               .then_inc(small_landed, 16)
            act.dma_start(gain_rows[G_Q:G_Q + KL, :], mla_q_norm.rearrange("l (k p) -> (l k) p", p=P))\
               .then_inc(small_landed, 16)
            act.dma_start(gain_rows[G_KV:G_KV + KL, :], mla_kv_norm.rearrange("l (k p) -> (l k) p", p=P))\
               .then_inc(small_landed, 16)
            act.wait_ge(angles_done, 1)
            R2 = ROPE // 2
            act.activation(rope_s[:, :, R2:], red_s[:, :, :], ACT.Sin).then_inc(sin_done, 1)
            act.activation(rope_c[:, :, 0:R2], red_c[:, :, :], ACT.Sin).then_inc(sin_done, 1)
            act.activation(rope_c[:, :, R2:], red_c[:, :, :], ACT.Sin).then_inc(sin_done, 1)
            act.preload_act_table_set("natural_log_exp_and_others")
            for j in range(LA):
                cut((bodies["win"], 0, j))
            act.wait_ge(gain_done, 1)
            turned_h("win", 0, G_ATTN[0])
            turned_h("win", 1, G_ATTN[0])

            small_junk = [pb[:, m, :].bitcast(BF16)[:, 0:LORA] for m in range(M)]

            def side_win(b, it, j):
                phase_start("win", N_ATTN0, G_ATTN[0], j)
                if j == 7:
                    chunk_full(b, it, j)
                    act.wait_ge(rstd_done, N_ATTN0 + 1)
                    act.activation(sg[:, 0, :], acc[0][0][:, :], ACT.Copy, scale=rstd[:, 0:1])\
                       .then_inc(acc_free[0][0], 1)
                if j == 8:
                    act.wait_ge(acc_free[0][0], 1)
                    act.wait_ge(acc_free[0][1], 1)
                    squares(N_Q, sg, small_junk)
                if j == 9:
                    root(N_Q)
                    turned_hi(0, TP0["lat"] + 1, None, ct_hi[:, 0:2, :], G_Q)
                    turned_hi(1, TP1["lat"] + 1, None, ct_hi[:, 2:4, :], G_Q + 2)
                if j == 15:
                    chunk_full(b, it, j)
                    act.activation(hm[:, 0, :], acc[1][0][:, :], ACT.Copy, scale=rstd[:, 0:1])\
                       .then_inc(acc_free[1][0], 1)
                if j == 16:
                    act.wait_ge(acc_free[1][0], 1)
                    act.wait_ge(acc_free[1][1], 1)
                    squares(N_KV, hm, small_junk)

            def mla_attention(g, j):
                v0, v1 = g * 5 + TP0["mla"], g * 4 + TP1["mla"]

                def q_k(x_):
                    act.wait_ge(tp_full[(x_ + 1) % 2], (v1, v0)[x_ % 2] + (1, 2, 2, 3)[x_])
                    act.activation(qkt[:, x_, :, :], tp[(x_ + 1) % 2][:, :].rearrange("p (s c) -> p s c", s=2),
                                   ACT.Copy).then_inc(tp_free[(x_ + 1) % 2], 1)

                def exps(x_):
                    act.wait_ge(max_done, g * GH + (x_ + 1))
                    a = x_ % 2
                    act.activation(pb[:, a, 0:P], sc[:, 0:P], ACT.Exp, bias=nmax_s[:, a, 0:1], scale=MLA_SCALE,
                                   accum_out=psums[:, a, 0:1])
                    act.activation(pb[:, a, P:3 * P], sc[:, P:3 * P], ACT.Exp, bias=nmax_s[:, a, 1:2],
                                   scale=MLA_SCALE, accum_out=psums[:, a, 1:2]).then_inc(exp_done, 1)

                if j == 0:
                    q_k(0)
                elif j == 1:
                    q_k(1)
                    q_k(2)
                    exps(0)
                elif j == 2:
                    q_k(3)
                    exps(1)
                elif j == 3:
                    exps(2)
                elif j == 4:
                    exps(3)
                if 3 <= j <= 6:
                    out_hi(g * GH + (j - 3), ot_slot(g, j - 3))

            def ot_slot(g, x_):
                return bass.ds(g * GH + x_, 1)

            def out_hi(head, slot):
                act.wait_ge(pv_full, head + 1)
                act.activation(ot_hi[:, slot, :], pv[:, 0:M * P], ACT.Copy).then_inc(o_hi_done, 1)

            def mla_take(b, it, j, g):
                if j == 2:
                    chunk_full(b, it, j)
                    q_ = qg[:, 0, :, :].rearrange("p h c -> p (h c)")
                    act.activation(q_[:, 0:CW], acc[0][0][:, :], ACT.Copy, scale=rstd_q[:, 0:1])\
                       .then_inc(acc_free[0][0], 1)
                    act.activation(q_[:, CW:], acc[1][0][:, 0:256], ACT.Copy, scale=rstd_q[:, 0:1])\
                       .then_inc(acc_free[1][0], 1)
                if j in (4, 6):
                    a = (j - 4) // 2
                    chunk_full(b, it, j)
                    act.activation(kvg[:, 0, 2 * a:2 * a + 2, :].rearrange("p h c -> p (h c)"),
                                   acc[a][0][:, :], ACT.Copy, scale=rstd_kv[:, 0:1])\
                       .then_inc(acc_free[a][0], 1)

            def side_mla0(b, it, j):
                if j == 0:
                    root(N_KV)
                    turned_hi(0, TP0["lat"] + 2, None, ct_hi[:, 4:6, :], G_KV)
                    turned_hi(1, TP1["lat"] + 2, None, ct_hi[:, 6:8, :], G_KV + 2)
                if j == 1:
                    act.wait_ge(tp_full[0], TP0["lat"] + 3)
                    act.activation(krt[:, :, :], tp[0][:, :].rearrange("p (s c) -> p s c", s=2), ACT.Copy)\
                       .then_inc(tp_free[0], 1)
                    act.wait_ge(rstd_done, N_KV + 1)
                mla_take(b, it, j, 0)

            def side_mla(b, it, j):
                mla_attention(it, j)
                mla_take(b, it, j, it + 1)

            def side_wo0(b, it, j):
                mla_attention(GROUPS - 1, j)

            def side_none(b, it, j):
                pass

            def silu(layer, b, it, c):
                chunk_full(b, it, 7)
                for m in range(M):
                    act.wait_ge(acc_free[1][m], c + ACC1[f"gu{layer}"])
                    act.activation(sg[:, m, :], acc[0][m][:, :], ACT.Silu, scale=rstd[:, m:m + 1])\
                       .then_inc(acc_free[0][m], 1)

            def hidden_hi(layer, c, u):
                turned_hi(u, c + ((TP0, TP1)[u][f"pair{layer}"] + 1), None,
                          hid_hi[:, bass.ds(c * 4 + 2 * u, 2), :], None)

            def ffn(layer):
                norm = (N_FFN0, N_FFN1)[layer]
                gu = f"gu{layer}"
                act.wait_ge(acc_free[1][0], ACC1[gu])
                act.wait_ge(acc_free[1][1], ACC1[gu])
                turned_h(gu, 0, G_FFN[layer])
                turned_h(gu, 1, G_FFN[layer])

                def side_first(b, it, j):
                    phase_start(gu, norm, G_FFN[layer], j)
                    if j == 7:
                        act.wait_ge(rstd_done, norm + 1)
                        silu(layer, b, it, 0)

                def side_gu(b, it, j):
                    if j in (1, 2):
                        hidden_hi(layer, it, j - 1)
                    if j == 7:
                        silu(layer, b, it, it + 1)

                run(f"gu{layer}a", side_first)
                run(gu, side_gu)
                hidden_hi(layer, PAIRS - 1, 0)
                hidden_hi(layer, PAIRS - 1, 1)

            def sb_attention(g, j):
                def head(x_):
                    return g * GH + x_
                if j < 4:
                    act.wait_ge(tp_full[0], g * GH + (TP0["sba"] + j + 1))
                    act.activation(qkt[:, j, :, :], tp[0][:, :].rearrange("p (s c) -> p s c", s=2), ACT.Copy)\
                       .then_inc(tp_free[0], 1)
                x_ = j - 1
                if 0 <= x_ < GH:
                    a, z = x_ % 2, zb[x_ % 2][:, 0:3 * P]
                    act.wait_ge(z_full, head(x_) + 1)
                    act.activation(sabs[:, a, :], z, ACT.Abs).then_inc(abs_done, 1)
                    act.wait_ge(abs_done, head(x_) + 1)
                    act.activation(sexp[:, a, :], sabs[:, a, :], ACT.Exp, scale=-1.0).then_inc(sexp_done, 1)
                    act.wait_ge(sexp_done, head(x_) + 1)
                    act.activation(sln[:, a, :], sexp[:, a, :], ACT.Ln, bias=1.0).then_inc(sln_done, 1)
                x_ = j - 3
                if 0 <= x_ < GH:
                    out_hi(head(x_) + HEADS, ot_slot(g, x_))
                x_ = j - 2
                if 0 <= x_ < GH:
                    act.wait_ge(logw_full, head(x_) + 1)
                    act.activation(pt[:, x_ % 2, :], zb[x_ % 2][:, 0:3 * P], ACT.Exp).then_inc(a_exp_done, 1)

            def sb_take(b, it, j):
                if j % 8 == 7:
                    c = j // 8
                    chunk_full(b, it, j)
                    act.activation((sq, sk, sv)[c][:, 0, :], acc[c % 2][0][:, :], ACT.Copy,
                                   scale=(rstd_q, rstd, rstd)[c][:, 0:1]).then_inc(acc_free[c % 2][0], 1)

            def side_sb0(b, it, j):
                phase_start("sb", N_ATTN1, G_ATTN[1], j)
                if j == 7:
                    act.wait_ge(rstd_done, N_ATTN1 + 1)
                    act.wait_ge(sb_scale_done, 1)
                sb_take(b, it, j)

            def side_sb(b, it, j):
                sb_attention(it, j)
                sb_take(b, it, j)

            run("win", side_win)
            run("mla0", side_mla0)
            run("mla", side_mla)
            run("wo0a", side_wo0)
            run("wo0b", side_none)
            ffn(0)
            run("down0", side_none)
            act.preload_act_table_set("natural_log_exp_and_others")
            act.wait_ge(acc_free[1][0], ACC1["sb"])
            act.wait_ge(acc_free[1][1], ACC1["sb"])
            turned_h("sb", 0, G_ATTN[1])
            turned_h("sb", 1, G_ATTN[1])
            run("sb0", side_sb0)
            run("sb", side_sb)
            run("wo1a", lambda b, it, j: sb_attention(GROUPS - 1, j))
            run("wo1b", side_none)
            ffn(1)
            run("down1a", side_none)
            run("down1b", side_none)
            act.preload_act_table_set("natural_log_exp_and_others")
            for m in range(M):
                act.wait_ge(acc_free[1][m], ACC1["end"])
            squares(N_FINAL, h, junk)
            root(N_FINAL)
            out_v = out[0].rearrange("(m p) d -> p m d", p=P)
            for n in range(2 * M):
                m, c = n // 2, n % 2
                act.wait_ge(out_ready, n + 1)
                act.dma_start(out_v[:, m, c * HW:(c + 1) * HW], h[:, m, c * HW:(c + 1) * HW])\
                   .then_inc(out_stored, 16)
            act.wait_ge(out_stored, 16 * 2 * M)

        @block.vector
        def _(dve):
            steps = [0]

            def chain(ins):
                steps[0] += 1
                ins.then_inc(dve_step, 1)
                dve.wait_ge(dve_step, steps[0])

            def cut(target):
                if target is None:
                    return
                b, it, j = target
                dve.wait_ge(hi_done, st.number(b, it, j) + 1)
                dve.tensor_tensor(w_lo[:, j % CUT, :], w_raw[:, j % RAW, :], w_hi[:, j % CUT, :].bitcast(F32),
                                  ALU.subtract).then_inc(lo_done, 1)

            def run(name, side):
                b = bodies[name]
                if b.iters == 1:
                    for j in range(b.n):
                        cut(st.ahead(b, 0, j))
                        side(b, 0, j)
                else:
                    with dve.Fori(0, b.iters) as it:
                        for j in range(b.n):
                            cut(st.ahead(b, it, j))
                            side(b, it, j)

            def chunk_full(b, it, j):
                dve.wait_ge(half_used, st.number(b, it, j) + 1)

            def turned_lo(u, count, lo, hi, gains):
                dve.wait_ge(t_hi_done, count)
                if gains is None:
                    dve.tensor_tensor(lo, tp[u][:, :].rearrange("p (t c) -> p t c", t=2), hi.bitcast(F32),
                                      ALU.subtract).then_inc(tp_free[u], 1)
                else:
                    for n in range(2):
                        ins = dve.scalar_tensor_tensor(
                            out=lo[:, n, :], in0=tp[u][:, n * M * P:(n + 1) * M * P],
                            scalar=gain[:, gains + n:gains + n + 1], in1=hi[:, n, :].bitcast(F32),
                            op0=ALU.mult, op1=ALU.subtract)
                    ins.then_inc(tp_free[u], 1)

            def turned_h(phase, u, g0):
                turned_lo(u % 2, THI[phase] + u + 1, xt_lo[:, 2 * u:2 * u + 2, :], xt_hi[:, 2 * u:2 * u + 2, :],
                          g0 + 2 * u)

            def mean_square(norm, width):
                dve.wait_ge(ssq_done, M * (norm + 1))
                dve.tensor_scalar(ms[:, :], ssq[:, :], 1.0 / width, EPS, ALU.mult, ALU.add).then_inc(ms_done, 1)

            def refine(norm, out_):
                dve.wait_ge(y0_done, norm + 1)
                if norm:
                    dve.wait_ge(rstd_done, norm)
                chain(dve.tensor_tensor(nt[:, :], y0[:, :], y0[:, :], ALU.mult))
                chain(dve.tensor_tensor(nt[:, :], nt[:, :], ms[:, :], ALU.mult))
                chain(dve.tensor_scalar(nt[:, :], nt[:, :], -0.5, 1.5, ALU.mult, ALU.add))
                dve.tensor_tensor(out_[:, :], y0[:, :], nt[:, :], ALU.mult).then_inc(rstd_done, 1)

            def phase_start(phase, norm, g0, j):
                if j + 2 < 8:
                    turned_h(phase, j + 2, g0)
                if j == 2:
                    mean_square(norm, D)
                if j == 4:
                    refine(norm, rstd)

            R2 = ROPE // 2
            TWO_PI = 2.0 * np.pi
            C1 = 6.28125
            C2 = float(np.float32(np.round((TWO_PI - C1) * 2.0 ** 21) / 2.0 ** 21))
            C3 = TWO_PI - C1 - C2
            ROUND = 1.5 * 2.0 ** 23
            PI_LESS = 3.1415925
            dve.wait_ge(pos_landed, 32)
            chain(dve.tensor_copy(pos_f[:, :], pos_i[:, :]))
            for m in range(M):
                ins = dve.tensor_scalar(ang[:, m, :], inv_f[:, :], pos_f[:, m:m + 1], None, ALU.mult)
            chain(ins)
            chain(dve.tensor_scalar(turns[:, :, :], ang[:, :, :], 1.0 / TWO_PI, ROUND, ALU.mult, ALU.add))
            chain(dve.tensor_scalar(turns[:, :, :], turns[:, :, :], ROUND, None, ALU.subtract))
            for c in (C1, C2, C3):
                chain(dve.scalar_tensor_tensor(out=ang[:, :, :], in0=turns[:, :, :], scalar=-c, in1=ang[:, :, :],
                                               op0=ALU.mult, op1=ALU.add))
            chain(dve.tensor_scalar(red_c[:, :, :], ang[:, :, :], np.pi / 2, None, ALU.add))
            chain(dve.tensor_scalar(turns[:, :, :], red_c[:, :, :], np.pi, -TWO_PI, ALU.is_gt, ALU.mult))
            chain(dve.tensor_tensor(red_c[:, :, :], red_c[:, :, :], turns[:, :, :], ALU.add))
            chain(dve.tensor_scalar(red_c[:, :, :], red_c[:, :, :], PI_LESS, -PI_LESS, ALU.min, ALU.max))
            dve.tensor_scalar(red_s[:, :, :], ang[:, :, :], PI_LESS, -PI_LESS, ALU.min, ALU.max)\
               .then_inc(angles_done, 1)
            dve.wait_ge(gain_full, 1)
            dve.tensor_copy(gain[:, :], sc[:, 0:NG]).then_inc(gain_done, 1)
            dve.wait_ge(sin_done, 3)
            dve.tensor_scalar(rope_s[:, :, 0:R2], rope_s[:, :, R2:], -1.0, None, ALU.mult).then_inc(rope_ready, 1)
            for j in range(LA):
                cut((bodies["win"], 0, j))
            dve.wait_ge(gain_done, 1)
            turned_h("win", 0, G_ATTN[0])
            turned_h("win", 1, G_ATTN[0])

            def turn_by_angles(x_, m, heads, step_sem, before, outs, done):
                cos = rope_c[:, m, :].unsqueeze(1).broadcast_to([P, heads, ROPE])
                sin = rope_s[:, m, :].unsqueeze(1).broadcast_to([P, heads, ROPE])
                t1, t2 = r_t1[:, m, 0:heads, :], r_t2[:, m, 0:heads, :]
                dve.tensor_tensor(t1, x_, cos, ALU.mult).then_inc(step_sem, 1)
                dve.tensor_tensor(t2[:, :, 0:R2], x_[:, :, R2:], sin[:, :, 0:R2], ALU.mult).then_inc(step_sem, 1)
                dve.tensor_tensor(t2[:, :, R2:], x_[:, :, 0:R2], sin[:, :, R2:], ALU.mult).then_inc(step_sem, 1)
                dve.wait_ge(step_sem, before + 3)
                for o in outs:
                    dve.tensor_tensor(o, t1, t2, ALU.add).then_inc(done, 1)

            def side_win(b, it, j):
                phase_start("win", N_ATTN0, G_ATTN[0], j)
                if j == 7:
                    chunk_full(b, it, j)
                    dve.wait_ge(rstd_done, N_ATTN0 + 1)
                    dve.tensor_scalar(sg[:, 1, :], acc[0][1][:, :], rstd[:, 1:2], None, ALU.mult)\
                       .then_inc(acc_free[0][1], 1)
                if j == 8:
                    mean_square(N_Q, LORA)
                if j == 9:
                    turned_lo(0, THI["lat"] + 1, ct_lo[:, 0:2, :], ct_hi[:, 0:2, :], G_Q)
                    turned_lo(1, THI["lat"] + 2, ct_lo[:, 2:4, :], ct_hi[:, 2:4, :], G_Q + 2)
                    refine(N_Q, rstd_q)
                if j == 15:
                    chunk_full(b, it, j)
                    dve.tensor_scalar(hm[:, 1, :], acc[1][1][:, :], rstd[:, 1:2], None, ALU.mult)\
                       .then_inc(acc_free[1][1], 1)
                if j == 16:
                    mean_square(N_KV, LORA)
                    chunk_full(b, it, j)
                    for m in range(M):
                        dve.tensor_scalar(kr[:, m, :], acc[0][m][:, 0:ROPE], rstd[:, m:m + 1], None, ALU.mult)\
                           .then_inc(acc_free[0][m], 1)
                    dve.wait_ge(rope_ready, 1)
                    for m in range(M):
                        dve.wait_ge(acc_free[0][m], 2)
                        turn_by_angles(kr[:, m:m + 1, :], m, 1, kr_step, 3 * m,
                                       [kr_pad[:, 0, m:m + 1, 0:ROPE], kr_pad[:, 1, m:m + 1, ROPE:]], kr_done)

            def out_lo(head, slot):
                dve.wait_ge(o_hi_done, head + 1)
                dve.tensor_tensor(ot_lo[:, slot, :], pv[:, 0:M * P], ot_hi[:, slot, :].bitcast(F32),
                                  ALU.subtract).then_inc(pv_free, 1)

            def mla_attention(g, j):
                v0, v1 = g * 5 + TP0["mla"], g * 4 + TP1["mla"]

                def head(x_):
                    return g * GH + x_

                def maxima(x_):
                    a = x_ % 2
                    dve.wait_ge(sc_full, head(x_) + 1)
                    dve.tensor_reduce(nmax[:, a, 0:1], sc[:, 0:P], AX_X, ALU.max).then_inc(nmax_done, 1)
                    dve.tensor_reduce(nmax[:, a, 1:2], sc[:, P:3 * P], AX_X, ALU.max).then_inc(nmax_done, 1)
                    dve.wait_ge(nmax_done, g * (2 * GH) + 2 * (x_ + 1))
                    dve.tensor_scalar(nmax_s[:, a, :], nmax[:, a, :], -MLA_SCALE, None, ALU.mult)\
                       .then_inc(max_done, 1)

                def normalise(x_):
                    a = x_ % 2
                    dve.wait_ge(exp_done, head(x_) + 1)
                    dve.reciprocal(prec[:, a, :], psums[:, a, :]).then_inc(prec_done, 1)
                    dve.wait_ge(prec_done, head(x_) + 1)
                    dve.tensor_scalar(pb[:, a, 0:P], pb[:, a, 0:P], prec[:, a, 0:1], None, ALU.mult)
                    dve.tensor_scalar(pb[:, a, P:3 * P], pb[:, a, P:3 * P], prec[:, a, 1:2], None, ALU.mult)\
                       .then_inc(p_done, 1)

                def take_p(x_):
                    dve.wait_ge(tp_full[(x_ + 1) % 2], (v1, v0)[x_ % 2] + (3, 4, 4, 5)[x_])
                    dve.tensor_copy(pt[:, x_ % 2, :], tp[(x_ + 1) % 2][:, 0:3 * P])\
                       .then_inc(tp_free[(x_ + 1) % 2], 1)

                if j == 0:
                    dve.wait_ge(tp_full[0], v0 + 1)
                    dve.tensor_copy(qrt[:, :, :], tp[0][:, :].rearrange("p (s c) -> p s c", s=2))\
                       .then_inc(tp_free[0], 1)
                elif j == 1:
                    maxima(0)
                    normalise(0)
                elif j == 2:
                    maxima(1)
                    take_p(0)
                    normalise(1)
                elif j == 3:
                    maxima(2)
                    take_p(1)
                    out_lo(head(0), bass.ds(head(0), 1))
                    normalise(2)
                elif j == 4:
                    maxima(3)
                    take_p(2)
                    out_lo(head(1), bass.ds(head(1), 1))
                    normalise(3)
                elif j == 5:
                    take_p(3)
                    out_lo(head(2), bass.ds(head(2), 1))
                elif j == 6:
                    out_lo(head(3), bass.ds(head(3), 1))

            def mla_take(b, it, j, g):
                if j == 2:
                    chunk_full(b, it, j)
                    q_ = qg[:, 1, :, :].rearrange("p h c -> p (h c)")
                    dve.tensor_scalar(q_[:, 0:CW], acc[0][1][:, :], rstd_q[:, 1:2], None, ALU.mult)\
                       .then_inc(acc_free[0][1], 1)
                    dve.tensor_scalar(q_[:, CW:], acc[1][1][:, 0:256], rstd_q[:, 1:2], None, ALU.mult)\
                       .then_inc(acc_free[1][1], 1)
                if j == 3:
                    for m in range(M):
                        dve.wait_ge(acc_free[0][m], g * 2 + ACC0["mla"] + 1)
                        dve.wait_ge(acc_free[1][m], g * 2 + ACC1["mla"] + 1)
                        qr = qg[:, m, :, NOPE:NOPE + ROPE]
                        turn_by_angles(qr, m, GH, q_step, g * 6 + 3 * m, [qrg[:, m, :, :]], q_rope)
                if j in (4, 6):
                    a = (j - 4) // 2
                    chunk_full(b, it, j)
                    dve.tensor_scalar(kvg[:, 1, 2 * a:2 * a + 2, :].rearrange("p h c -> p (h c)"),
                                      acc[a][1][:, :], rstd_kv[:, 1:2], None, ALU.mult)\
                       .then_inc(acc_free[a][1], 1)

            def side_mla0(b, it, j):
                if j == 0:
                    turned_lo(0, THI["lat"] + 3, ct_lo[:, 4:6, :], ct_hi[:, 4:6, :], G_KV)
                    turned_lo(1, THI["lat"] + 4, ct_lo[:, 6:8, :], ct_hi[:, 6:8, :], G_KV + 2)
                    refine(N_KV, rstd_kv)
                if j == 1:
                    dve.wait_ge(rstd_done, N_KV + 1)
                mla_take(b, it, j, 0)

            def side_mla(b, it, j):
                mla_attention(it, j)
                mla_take(b, it, j, it + 1)

            def add_chunk(b, it, j, a, n):
                chunk_full(b, it, j)
                cols = bass.ds(n * CW, CW)
                for m in range(M):
                    dve.tensor_tensor(h[:, m, cols], acc[a][m][:, :], h[:, m, cols], ALU.add)\
                       .then_inc(acc_free[a][m], 1)

            def wo_adds(n):
                def adds(b, it, j):
                    if j % 8 == 7:
                        add_chunk(b, it, j, j // 8, n + j // 8)
                return adds

            def down_adds(n):
                def adds(b, it, j):
                    if j % 22 == 21:
                        add_chunk(b, it, j, j // 22, it * 2 + n + j // 22)
                return adds

            def times_up(layer, b, it, c):
                chunk_full(b, it, 15)
                for m in range(M):
                    dve.wait_ge(acc_free[0][m], c + (ACC0[f"gu{layer}"] + 1))
                    dve.scalar_tensor_tensor(out=hm[:, m, :], in0=acc[1][m][:, :], scalar=rstd[:, m:m + 1],
                                             in1=sg[:, m, :], op0=ALU.mult, op1=ALU.mult)\
                       .then_inc(acc_free[1][m], 1)

            def hidden_lo(layer, c, u):
                k = bass.ds(c * 4 + 2 * u, 2)
                turned_lo(u, c * 2 + (THI[f"pair{layer}"] + u + 1), hid_lo[:, k, :], hid_hi[:, k, :], None)

            def ffn(layer):
                norm = (N_FFN0, N_FFN1)[layer]
                gu = f"gu{layer}"
                turned_h(gu, 0, G_FFN[layer])
                turned_h(gu, 1, G_FFN[layer])

                def side_first(b, it, j):
                    phase_start(gu, norm, G_FFN[layer], j)
                    if j == 15:
                        dve.wait_ge(rstd_done, norm + 1)
                        times_up(layer, b, it, 0)

                def side_gu(b, it, j):
                    if j in (1, 2):
                        hidden_lo(layer, it, j - 1)
                    if j == 15:
                        times_up(layer, b, it, it + 1)

                run(f"gu{layer}a", side_first)
                run(gu, side_gu)
                hidden_lo(layer, PAIRS - 1, 0)
                hidden_lo(layer, PAIRS - 1, 1)

            def sb_attention(g, j):
                def head(x_):
                    return g * GH + x_

                def diagonal(t_):
                    return t_.rearrange("p (n c) -> p n c", n=3)[:, 0:3:2, :]

                keep = strict[:, :].unsqueeze(1).broadcast_to([P, 2, P])
                x_ = j - 1
                if 0 <= x_ < GH:
                    a = x_ % 2
                    dve.wait_ge(sln_done, head(x_) + 1)
                    dve.scalar_tensor_tensor(out=ssp[:, a, :], in0=zb[a][:, 0:3 * P], scalar=0.0,
                                             in1=sln[:, a, :], op0=ALU.max, op1=ALU.add).then_inc(ssp_step, 1)
                    dve.wait_ge(ssp_step, head(x_) + 1)
                    s_ = diagonal(ssp[:, a, :])
                    dve.tensor_tensor(s_, s_, keep, ALU.mult).then_inc(ssp_done, 1)
                x_ = j - 3
                if 0 <= x_ < GH:
                    out_lo(head(x_) + HEADS, bass.ds(head(x_), 1))
                x_ = j - 2
                if 0 <= x_ < GH:
                    dve.wait_ge(a_exp_done, head(x_) + 1)
                    w_ = diagonal(pt[:, x_ % 2, :])
                    dve.scalar_tensor_tensor(out=w_, in0=w_, scalar=BIG, in1=keep, op0=ALU.min, op1=ALU.mult)\
                       .then_inc(a_done, 1)

            def sb_take(b, it, j):
                if j % 8 == 7:
                    c = j // 8
                    chunk_full(b, it, j)
                    dve.tensor_scalar((sq, sk, sv)[c][:, 1, :], acc[c % 2][1][:, :],
                                      (rstd_q, rstd, rstd)[c][:, 1:2], None, ALU.mult)\
                       .then_inc(acc_free[c % 2][1], 1)

            def side_sb0(b, it, j):
                phase_start("sb", N_ATTN1, G_ATTN[1], j)
                if j == 5:
                    dve.wait_ge(rstd_done, N_ATTN1 + 1)
                    dve.tensor_scalar(rstd_q[:, :], rstd[:, :], SB_SCALE, None, ALU.mult)\
                       .then_inc(sb_scale_done, 1)
                    dve.wait_ge(sb_scale_done, 1)
                sb_take(b, it, j)

            def side_sb(b, it, j):
                sb_attention(it, j)
                sb_take(b, it, j)

            run("win", side_win)
            run("mla0", side_mla0)
            run("mla", side_mla)

            def side_wo0(b, it, j):
                mla_attention(GROUPS - 1, j)
                wo_adds(0)(b, it, j)

            def side_wo1(b, it, j):
                sb_attention(GROUPS - 1, j)
                wo_adds(0)(b, it, j)

            run("wo0a", side_wo0)
            run("wo0b", wo_adds(2))
            ffn(0)
            run("down0", down_adds(0))
            turned_h("sb", 0, G_ATTN[1])
            turned_h("sb", 1, G_ATTN[1])
            run("sb0", side_sb0)
            run("sb", side_sb)
            run("wo1a", side_wo1)
            run("wo1b", wo_adds(2))
            ffn(1)
            run("down1a", down_adds(0))
            run("down1b", down_adds(2))
            mean_square(N_FINAL, D)
            refine(N_FINAL, rstd)
            dve.wait_ge(rstd_done, N_FINAL + 1)
            dve.wait_ge(gfin_landed, 16)
            for n in range(2 * M):
                m, c = n // 2, slice((n % 2) * HW, (n % 2 + 1) * HW)
                dve.scalar_tensor_tensor(out=h[:, m, c], in0=h[:, m, c], scalar=rstd[:, m:m + 1],
                                         in1=gfin[:, c], op0=ALU.mult, op1=ALU.mult).then_inc(out_ready, 1)


_INS = ["x", "positions", "attn_norm", "mla_w_in", "mla_q_norm", "mla_kv_norm", "mla_w_uq", "mla_w_ukv",
        "mla_w_o", "sb_w_in", "sb_w_o", "ffn_norm", "ffn_w_gate_up", "ffn_w_down", "final_norm"]


def kernel(**inputs):
    import concourse.bacc as _bacc
    from concourse.bass_utils import run_bass_kernel_spmd as _run

    nc = _bacc.Bacc("TRN2", target_bir_lowering=False, num_devices=1, dynamic_dma_scratch_size=1024)
    arrays, args = {}, []
    values = {name: np.ascontiguousarray(inputs[name]) for name in _INS}
    values["inv_freq"] = (np.float32(THETA) ** (-np.arange(0, ROPE, 2, dtype=np.float32) / np.float32(ROPE)))
    for name, a in values.items():
        arrays[f"in_{name}_dram"] = a
        args.append(nc.dram_tensor(f"in_{name}_dram", a.shape, mybir.dt.from_np(a.dtype), kind="ExternalInput").ap())
    out = nc.dram_tensor("out_0_dram", (1, M * P, D), F32, kind="ExternalOutput").ap()
    trunk(nc, *args, out)
    r = _run(nc, [arrays], core_ids=[0])
    return r.results[0]["out_0_dram"]
```

```python
from contextlib import ExitStack

import numpy as np

import concourse.bass as bass
from concourse import mybir

F32 = mybir.dt.float32
F32R = mybir.dt.float32r
BF16 = mybir.dt.bfloat16
I32 = mybir.dt.int32
ACT = mybir.ActivationFunctionType
ALU = mybir.AluOpType
AX_X = mybir.AxisListType.X

P = 128
M = 2
D = 2048
KD = D // P
LORA = 512
KL = LORA // P
NOPE, ROPE, VD = 128, 64, 128
HEADS, GH = 16, 4
GROUPS = HEADS // GH
FF = 5632
KF = FF // P
CW = 512
PAIRS = FF // CW
HW = 1024
RAW, CUT = 8, 4
LA = 3
EPS = 1e-6
MLA_SCALE = float(NOPE + ROPE) ** -0.5
SB_SCALE = float(128) ** -0.5
MASKED = -1e30
BIG = 3.0e38
THETA = 10000.0


class Body:

    def __init__(self, name, n, iters=1, slot0=0):
        self.name, self.n, self.iters, self.slot0 = name, n, iters, slot0

    def raw(self, j):
        return (self.slot0 + j) % RAW

    def cut(self, j):
        return (self.slot0 + j) % CUT


class Stream:

    def __init__(self, bodies):
        self.bodies = bodies
        count, fills = 0, [0] * RAW
        last_raw, last_cut = {}, {}
        for b in bodies:
            b.base, b.fills = count, list(fills)
            b.per = [sum(b.raw(j) == s for j in range(b.n)) for s in range(RAW)]
            b.raw_gap, b.cut_gap = {}, {}
            for it in range(b.iters):
                for j in range(b.n):
                    r = b.base + it * b.n + j
                    if b.raw(j) in last_raw:
                        b.raw_gap[j] = min(b.raw_gap.get(j, RAW), r - last_raw[b.raw(j)])
                    if b.cut(j) in last_cut:
                        b.cut_gap[j] = min(b.cut_gap.get(j, CUT), r - last_cut[b.cut(j)])
                    last_raw[b.raw(j)] = last_cut[b.cut(j)] = r + 1
            count += b.iters * b.n
            fills = [f + b.iters * q for f, q in zip(fills, b.per)]
        for b, nxt in zip(bodies, bodies[1:]):
            if b.iters > 1:
                for j in range(LA):
                    assert b.slot0 == nxt.slot0 == 0
                    assert b.base + b.iters * b.n == nxt.base and b.fills[j] + b.iters * b.per[j] == nxt.fills[j]
                    b.cut_gap[j] = min(b.cut_gap[j], nxt.cut_gap[j])

    def ahead(self, b, it, j):
        if j + LA < b.n:
            return b, it, j + LA
        if b.iters > 1:
            return b, it + 1, j + LA - b.n
        k = self.bodies.index(b) + 1
        return (self.bodies[k], 0, j + LA - b.n) if k < len(self.bodies) else None

    def number(self, b, it, j):
        return it * b.n + (b.base + j)

    def landed(self, b, it, j):
        return it * (16 * b.per[b.raw(j)]) + 16 * (b.fills[b.raw(j)] + j // RAW + 1)


def trunk(nc, x, positions, attn_norm, mla_w_in, mla_q_norm, mla_kv_norm, mla_w_uq, mla_w_ukv,
          mla_w_o, sb_w_in, sb_w_o, ffn_norm, ffn_w_gate_up, ffn_w_down, final_norm, inv_freq, out):
    bodies = {
        "win": Body("win", 17, slot0=7),
        "mla0": Body("mla0", 7), "mla": Body("mla", 7, GROUPS - 1),
        "wo0a": Body("wo0a", 16), "wo0b": Body("wo0b", 16),
        "gu0a": Body("gu0a", 16), "gu0": Body("gu0", 16, PAIRS - 1),
        "down0a": Body("down0a", 44), "down0b": Body("down0b", 44),
        "sb0": Body("sb0", 24), "sb": Body("sb", 24, GROUPS - 1),
        "wo1a": Body("wo1a", 16), "wo1b": Body("wo1b", 16),
        "gu1a": Body("gu1a", 16), "gu1": Body("gu1", 16, PAIRS - 1),
        "down1a": Body("down1a", 44), "down1b": Body("down1b", 44),
    }
    st = Stream(list(bodies.values()))

    def rows(w, k, n, c0, cols):
        return w[k * P:(k + n) * P, bass.ds(c0, cols)].rearrange("(t p) c -> p t c", p=P)

    w_in, w_uq, w_ukv = mla_w_in[0], mla_w_uq[0], mla_w_ukv[0]
    HQ = GH * (NOPE + ROPE)
    HKV = GH * (NOPE + VD)

    KR_HALF = 12
    WIN = [(0, k) for k in range(8)] + [(1, k) for k in range(8)]
    WIN.insert(KR_HALF, (2, 0))
    WO = [(0, k) for k in range(7)] + [(1, 0), (0, 7)] + [(1, k) for k in range(1, 8)]
    SB = [(0, k) for k in range(8)] + [(1, 0), (1, 1)] + [(2, k) for k in range(8)] + \
        [(1, k) for k in range(2, 8)]

    def src_win(it, j):
        c, k = WIN[j]
        return rows(w_in, 2 * k, 2, CW * c, CW) if c < 2 else rows(w_in, 0, KD, 2 * LORA, ROPE)

    def src_mla(g):
        def src(it, j):
            if j < 2:
                return rows(w_uq, 2 * j, 2, (it + g) * HQ, CW)
            if j == 2:
                return rows(w_uq, 0, KL, (it + g) * HQ + CW, HQ - CW)
            return rows(w_ukv, 2 * ((j - 3) % 2), 2, (it + g) * HKV + CW * ((j - 3) // 2), CW)
        return src

    def src_wo(w, n):
        return lambda it, j: rows(w, 2 * WO[j][1], 2, CW * (n + WO[j][0]), CW)

    def src_gu(w, c):
        return lambda it, j: rows(w, 2 * (j % 8), 2, (it + c) * CW + FF * (j // 8), CW)

    def src_down(w, c):
        return lambda it, j: rows(w, 2 * (j % 22), 2, (2 * it + c + j // 22) * CW, CW)

    def src_sb(g):
        return lambda it, j: rows(sb_w_in[0], 2 * SB[j][1], 2, (it + g) * CW + D * SB[j][0], CW)

    source = {
        "win": src_win, "mla0": src_mla(0), "mla": src_mla(1),
        "wo0a": src_wo(mla_w_o[0], 0), "wo0b": src_wo(mla_w_o[0], 2),
        "gu0a": src_gu(ffn_w_gate_up[0], 0), "gu0": src_gu(ffn_w_gate_up[0], 1),
        "down0a": src_down(ffn_w_down[0], 0), "down0b": src_down(ffn_w_down[0], 2),
        "sb0": src_sb(0), "sb": src_sb(1),
        "wo1a": src_wo(sb_w_o[0], 0), "wo1b": src_wo(sb_w_o[0], 2),
        "gu1a": src_gu(ffn_w_gate_up[1], 0), "gu1": src_gu(ffn_w_gate_up[1], 1),
        "down1a": src_down(ffn_w_down[1], 0), "down1b": src_down(ffn_w_down[1], 2),
    }

    with ExitStack() as ctx:
        top = [nc.sbuf_base]

        def at(name, shape, dt, offset):
            return nc.alloc_sbuf_tensor_at(name, shape, dt, offset=offset)

        def size(shape, dt):
            return int(np.prod(shape[1:])) * (2 if dt == BF16 else 4)

        def sb(name, shape, dt):
            off = (top[0] + 63) // 64 * 64
            top[0] = off + size(shape, dt)
            return at(name, shape, dt, off)

        def sem(name):
            return ctx.enter_context(nc.semaphore(name))

        h = sb("h", [P, M, D], F32)
        xt_hi = sb("xt_hi", [P, KD, M * P], F32R)
        xt_lo = sb("xt_lo", [P, KD, M * P], F32R)
        gfin = at("gfin", [P, D], F32, top[0] - size([P, KD, M * P], F32R))
        w_raw = sb("w_raw", [P, RAW, HW], F32)
        w_hi = sb("w_hi", [P, CUT, HW], F32R)
        w_lo = sb("w_lo", [P, CUT, HW], F32R)
        area = (top[0] + 63) // 64 * 64
        hid_hi = sb("hid_hi", [P, KF, M * P], F32R)
        hid_lo = sb("hid_lo", [P, KF, M * P], F32R)
        area_end, area_top = top[0], [area]

        def part(name, shape, dt):
            off = area_top[0]
            area_top[0] += size(shape, dt)
            assert area_top[0] <= area_end
            return at(name, shape, dt, off)

        ot_hi = part("ot_hi", [P, HEADS, M * P], F32R)
        ot_lo = part("ot_lo", [P, HEADS, M * P], F32R)
        qkt = part("qkt", [P, GH, 2, M * P], F32)
        pb = part("pb", [P, 2, 3 * P], F32)
        pt = part("pt", [P, 2, 3 * P], F32)
        mixer_top = area_top[0]
        ct_hi = part("ct_hi", [P, 2 * KL, M * P], F32R)
        ct_lo = part("ct_lo", [P, 2 * KL, M * P], F32R)
        qg = part("qg", [P, M, GH, NOPE + ROPE], F32)
        qrg = part("qrg", [P, M, GH, ROPE], F32)
        kvg = part("kvg", [P, M, GH, NOPE + VD], F32)
        qrt = part("qrt", [P, 2, M * P], F32)
        area_top[0] = mixer_top
        sq = part("sq", [P, M, CW], F32)
        sk = part("sk", [P, M, CW], F32)
        sv = part("sv", [P, M, CW], F32)
        sabs = part("sabs", [P, 2, 3 * P], F32)
        sexp = part("sexp", [P, 2, 3 * P], F32)
        sln = part("sln", [P, 2, 3 * P], F32)
        ssp = part("ssp", [P, 2, 3 * P], F32)

        sg = sb("sg", [P, M, CW], F32)
        hm = sb("hm", [P, M, CW], F32)
        junk = [t_[:, :, :].rearrange("p m c -> p (m c)").bitcast(BF16) for t_ in (sg, hm)]
        ident = sb("ident", [P, P], F32)
        ident_h = sb("ident_h", [P, P], BF16)
        causal = sb("causal", [P, P], BF16)
        strict = sb("strict", [P, P], F32)
        neg_tri = sb("neg_tri", [P, P], F32)
        neg_one = sb("neg_one", [P, P], F32)
        NG = 4 * KD + 2 * KL
        gain_rows = sb("gain_rows", [NG, P], F32)
        gain = sb("gain", [P, NG], F32)
        pos_i = sb("pos_i", [P, M], I32)
        pos_f = sb("pos_f", [P, M], F32)
        inv_f = sb("inv_f", [P, ROPE // 2], F32)
        ang = sb("ang", [P, M, ROPE // 2], F32)
        turns = sb("turns", [P, M, ROPE // 2], F32)
        red_s = sb("red_s", [P, M, ROPE // 2], F32)
        red_c = sb("red_c", [P, M, ROPE // 2], F32)
        rope_c = sb("rope_c", [P, M, ROPE], F32)
        rope_s = sb("rope_s", [P, M, ROPE], F32)
        r_t1 = sb("r_t1", [P, M, GH, ROPE], F32)
        r_t2 = sb("r_t2", [P, M, GH, ROPE], F32)
        kr = sb("kr", [P, M, ROPE], F32)
        kr_pad = sb("kr_pad", [P, 2, M, P], F32)
        krt = sb("krt", [P, 2, M * P], F32)
        ssq = sb("ssq", [P, M], F32)
        ssq_part = sb("ssq_part", [P, M, D // CW], F32)
        ms = sb("ms", [P, M], F32)
        ln_ms = sb("ln_ms", [P, M], F32)
        y0 = sb("y0", [P, M], F32)
        nt = sb("nt", [P, M], F32)
        rstd = sb("rstd", [P, M], F32)
        rstd_q = sb("rstd_q", [P, M], F32)
        rstd_kv = sb("rstd_kv", [P, M], F32)
        nmax = sb("nmax", [P, 2, M], F32)
        nmax_s = sb("nmax_s", [P, 2, M], F32)
        psums = sb("psums", [P, 2, M], F32)
        prec = sb("prec", [P, 2, M], F32)
        assert top[0] <= nc.sbuf_usable_end, (top[0], nc.sbuf_usable_end)

        def bank(name, shape):
            return ctx.enter_context(nc.psum_tensor(name, shape, F32))

        acc = [[bank(f"acc{a}{m}", [P, CW]) for m in range(M)] for a in range(2)]
        tp = [bank(f"tp{b}", [P, CW]) for b in range(2)]
        sc = bank("sc", [P, CW])
        pv = bank("pv", [P, CW])
        zb = [sc, tp[1]]

        landed = [sem(f"w_landed{s}") for s in range(RAW)]
        hi_done = sem("w_hi_done")
        lo_done = sem("w_lo_done")
        half_used = sem("w_half_used")
        x_landed = [sem(f"x_landed{c}") for c in range(D // CW)]
        attn_gains_landed = sem("attn_gains_landed")
        small_landed = sem("small_landed")
        gfin_landed = sem("gfin_landed")
        consts_done = sem("consts_done")
        pool_step = sem("pool_step")
        gain_full = sem("gain_full")
        gain_done = sem("gain_done")
        acc_free = [[sem(f"acc{a}{m}_free") for m in range(M)] for a in range(2)]
        tp_full = [sem(f"tp{b}_full") for b in range(2)]
        tp_free = [sem(f"tp{b}_free") for b in range(2)]
        t_hi_done = sem("t_hi_done")
        ssq_done = sem("ssq_done")
        ms_done = sem("ms_done")
        ln_done = sem("ln_done")
        y0_done = sem("y0_done")
        rstd_done = sem("rstd_done")
        dve_step = sem("dve_step")
        rope_ready = sem("rope_ready")
        angles_done = sem("angles_done")
        sin_done = sem("sin_done")
        pos_landed = sem("pos_landed")
        kr_step = sem("kr_step")
        kr_done = sem("kr_done")
        q_step = sem("q_rope_step")
        sb_scale_done = sem("sb_scale_done")
        nmax_done = sem("nmax_done")
        prec_done = sem("prec_done")
        ssp_step = sem("ssp_step")
        gained = sem("gained")
        out_act = sem("out_ready_act")
        out_dve = sem("out_ready_dve")
        q_rope = sem("q_rope_done")
        sc_full = sem("scores_full")
        max_done = sem("max_done")
        exp_done = sem("exp_done")
        p_done = sem("p_normalised")
        pv_full = sem("pv_full")
        o_hi_done = sem("o_hi_done")
        pv_free = sem("pv_free")
        z_full = sem("z_full")
        abs_done = sem("abs_done")
        sexp_done = sem("sexp_done")
        sln_done = sem("softplus_ln_done")
        ssp_done = sem("softplus_done")
        logw_full = sem("log_weights_full")
        a_exp_done = sem("a_exp_done")
        a_done = sem("a_masked")
        out_stored = sem("out_stored")

        G_ATTN, G_FFN, G_Q, G_KV = (0, KD), (2 * KD, 3 * KD), 4 * KD, 4 * KD + KL

        block = ctx.enter_context(nc.Block())

        kr_turned = pt[0:ROPE, 0, 0:M * P]
        x_v = x[0].rearrange("(m p) d -> p m d", p=P)
        out_v = out[0].rearrange("(m p) d -> p m d", p=P)

        @block.sync
        def _(sp):
            def load_x(c):
                cols = slice(c * CW, (c + 1) * CW)
                sp.dma_start(h[:, :, cols], x_v[:, :, cols]).then_inc(x_landed[c], 16)

            load_x(0)

            def load(b, it):
                for j in range(b.n):
                    s = b.raw(j)
                    if j in b.raw_gap:
                        sp.wait_ge(lo_done, st.number(b, it, j) - b.raw_gap[j])
                    src = source[b.name](it, j)
                    dst = w_raw[:, s, :].rearrange("p (t c) -> p t c", t=src.shape[1])
                    sp.dma_start(dst, src).then_inc(landed[s], 16)
                    if b.name == "win" and j in (3, 4):
                        load_x(j - 1)

            for b in st.bodies:
                if b.iters == 1:
                    load(b, 0)
                else:
                    with sp.Fori(0, b.iters) as it:
                        load(b, it)
                if b is bodies["down1a"]:
                    sp.wait_ge(half_used, st.number(b, 0, 0) + 1)
                    sp.dma_start(gfin[:, :],
                                 final_norm.partition_broadcast(P)).then_inc(gfin_landed, 16)
            for m in range(M):
                sp.wait_ge(out_dve, m + 1)
                sp.dma_start(out_v[:, m, HW:], h[:, m, HW:]).then_inc(out_stored, 16)

        @block.gpsimd
        def _(pool):
            pool.memset(ident[:, :], 0.0).then_inc(pool_step, 1)
            pool.memset(ident_h[:, :], 0.0).then_inc(pool_step, 1)
            pool.memset(causal[:, :], 0.0).then_inc(pool_step, 1)
            pool.memset(strict[:, :], 1.0).then_inc(pool_step, 1)
            pool.memset(neg_tri[:, :], -1.0).then_inc(pool_step, 1)
            pool.memset(neg_one[:, :], -1.0).then_inc(consts_done, 1)
            pool.memset(kr_pad[:, :, :, :], 0.0).then_inc(consts_done, 1)
            pool.wait_ge(pool_step, 5)
            for m in (ident, ident_h):
                pool.affine_select(out=m[:, :], in_=m[:, :], compare_op=ALU.not_equal, fill=1.0, base=0,
                                   pattern=[[-1, P]], channel_multiplier=1).then_inc(consts_done, 1)
            pool.affine_select(out=causal[:, :], in_=causal[:, :], compare_op=ALU.is_ge, fill=MASKED,
                               base=0, pattern=[[-1, P]], channel_multiplier=1).then_inc(consts_done, 1)
            pool.affine_select(out=strict[:, :], in_=strict[:, :], compare_op=ALU.is_gt, fill=0.0,
                               base=0, pattern=[[1, P]], channel_multiplier=-1).then_inc(consts_done, 1)
            pool.affine_select(out=neg_tri[:, :], in_=neg_tri[:, :], compare_op=ALU.is_ge, fill=0.0,
                               base=0, pattern=[[-1, P]], channel_multiplier=1).then_inc(consts_done, 1)
            pool.dma_start(gain_rows[G_Q:G_Q + KL, :], mla_q_norm.rearrange("l (k p) -> (l k) p", p=P))\
                .then_inc(small_landed, 16)
            pool.dma_start(gain_rows[G_KV:G_KV + KL, :], mla_kv_norm.rearrange("l (k p) -> (l k) p", p=P))\
                .then_inc(small_landed, 16)
            pool.dma_start(gain_rows[2 * KD:4 * KD, :], ffn_norm.rearrange("l (k p) -> (l k) p", p=P))\
                .then_inc(small_landed, 16)
            with nc.allow_non_contiguous_dma(reason="256 positions, once"):
                pool.dma_start(pos_i[:, :], positions.rearrange("b (m p) -> p (b m)", p=P))\
                    .then_inc(pos_landed, 16)
            pool.dma_start(inv_f[:, :], inv_freq.partition_broadcast(P)).then_inc(pos_landed, 16)

        CONSTS, SMALL = 7, 3

        ACC0 = {"win": 0, "mla": 2}
        ACC1 = {"win": 0, "mla": 1}
        ACC0["wo0"], ACC1["wo0"] = ACC0["mla"] + 2 * GROUPS, ACC1["mla"] + 2 * GROUPS
        ACC0["gu0"], ACC1["gu0"] = ACC0["wo0"] + 2, ACC1["wo0"] + 2
        ACC0["down0"], ACC1["down0"] = ACC0["gu0"] + PAIRS, ACC1["gu0"] + PAIRS
        ACC0["sb"], ACC1["sb"] = ACC0["down0"] + 2, ACC1["down0"] + 2
        ACC0["wo1"], ACC1["wo1"] = ACC0["sb"] + 2 * GROUPS, ACC1["sb"] + GROUPS
        ACC0["gu1"], ACC1["gu1"] = ACC0["wo1"] + 2, ACC1["wo1"] + 2
        ACC0["down1"], ACC1["down1"] = ACC0["gu1"] + PAIRS, ACC1["gu1"] + PAIRS
        ACC0["end"], ACC1["end"] = ACC0["down1"] + 2, ACC1["down1"] + 2
        UH = KD // 4
        TP0 = {"win": 0, "lat": UH, "mla": UH + 4}
        TP1 = {"win": 0, "lat": UH, "mla": UH + 2}
        TP0["gu0"], TP1["gu0"] = TP0["mla"] + 5 * GROUPS, TP1["mla"] + 4 * GROUPS
        TP0["pair0"], TP1["pair0"] = TP0["gu0"] + UH, TP1["gu0"] + UH
        TP0["sb"], TP1["sb"] = TP0["pair0"] + PAIRS, TP1["pair0"] + PAIRS
        TP0["sba"], TP1["sba"] = TP0["sb"] + UH, TP1["sb"] + UH
        TP0["gu1"], TP1["gu1"] = TP0["sba"] + GH * GROUPS, TP1["sba"]
        TP0["pair1"], TP1["pair1"] = TP0["gu1"] + UH, TP1["gu1"] + UH
        THI = {"win": 0, "lat": 2 * UH, "gu0": 2 * UH + 4}
        THI["pair0"] = THI["gu0"] + 2 * UH
        THI["sb"] = THI["pair0"] + 2 * PAIRS
        THI["gu1"] = THI["sb"] + 2 * UH
        THI["pair1"] = THI["gu1"] + 2 * UH
        N_ATTN0, N_Q, N_KV, N_FFN0, N_ATTN1, N_FFN1, N_FINAL = range(7)
        TAIL = CUT

        @block.tensor
        def _(pe):
            def products(b, it, j, a, hi, lo, k0, nk, n, c0=0, first=False, last=False, free=None,
                         tokens=range(M), used=1):
                if free is not None and not (isinstance(free, int) and free == 0):
                    for m in range(M):
                        pe.wait_ge(acc_free[a][m], free)
                pe.wait_ge(lo_done, st.number(b, it, j) + 1)
                wh = w_hi[:, b.cut(j), :].rearrange("p (t c) -> p t c", t=nk)
                wl = w_lo[:, b.cut(j), :].rearrange("p (t c) -> p t c", t=nk)
                for k in range(nk):
                    for m in tokens:
                        o = acc[a][m][:, c0:c0 + n]
                        xh = hi[:, k0 + k, m * P:(m + 1) * P]
                        xl = lo[:, k0 + k, m * P:(m + 1) * P]
                        pe.matmul(o, xh, wh[:, k, :], start=first and k == 0, stop=False)
                        pe.matmul(o, xh, wl[:, k, :], start=False, stop=False)
                        mm = pe.matmul(o, xl, wh[:, k, :], start=False, stop=last and k == nk - 1)
                if used:
                    mm.then_inc(half_used, used)

            def turn(b, before, tiles):
                if not (isinstance(before, int) and before == 0):
                    pe.wait_ge(tp_free[b], before)
                for n, tile in enumerate(tiles):
                    mm = pe.transpose(tp[b][:, n * P:(n + 1) * P], tile, ident[:, :])
                mm.then_inc(tp_full[b], 1)

            def tiles_of(src, k):
                return [src[:, m, kk * P:(kk + 1) * P] for kk in (k, k + 1) for m in range(M)]

            def turn_h(phase, u):
                for m in range(M):
                    if phase == "win":
                        pe.wait_ge(x_landed[u // 2], 16)
                    else:
                        pe.wait_ge(acc_free[u // 2 % 2][m], (ACC0, ACC1)[u // 2 % 2][phase] - 1 + u // 4)
                turn(u % 2, (TP0, TP1)[u % 2][phase] + u // 2, tiles_of(h, 2 * u))

            def turned_h(phase, u):
                pe.wait_ge(tp_free[u % 2], (TP0, TP1)[u % 2][phase] + u // 2 + 1)

            def first_chunk(phase, b, free):
                for j in range(8):
                    turned_h(phase, j)
                    products(b, 0, j, 0, xt_hi, xt_lo, 2 * j, 2, CW, first=j == 0, last=j == 7,
                             free=free if j == 0 else None)
                    if j + 2 < 8:
                        turn_h(phase, j + 2)

            def mla_scores(g, x_, v0, v1):
                pe.wait_ge(tp_free[(x_ + 1) % 2], (v1, v0)[x_ % 2] + (1, 2, 2, 3)[x_])
                if x_:
                    pe.wait_ge(exp_done, GH * g + x_)
                for m in range(M):
                    o, keys = sc[:, m * P:], (m + 1) * P
                    q = qkt[:, x_, 0, m * P:(m + 1) * P]
                    qr = qrt[:, x_ // 2, m * P:(m + 1) * P]
                    k_ = qkt[:, x_, 1, :]
                    kr_ = krt[:, x_ % 2, :]
                    pe.matmul(o[:, 0:keys], q, k_[:, 0:keys], start=True, stop=False, skip_group_check=True)
                    pe.matmul(o[:, 0:keys], qr, kr_[:, 0:keys], start=False, stop=False,
                              skip_group_check=True)
                    mm = pe.matmul(o[:, m * P:keys], ident_h[:, :], causal[:, :], start=False, stop=True,
                                   skip_group_check=True)
                mm.then_inc(sc_full, 1)

            def mla_turn_p(g, x_, v0, v1):
                pe.wait_ge(p_done, GH * g + x_ + 1)
                turn((x_ + 1) % 2, (v1, v0)[x_ % 2] + (2, 3, 3, 4)[x_],
                     [pb[:, x_ % 2, n * P:(n + 1) * P] for n in range(3)])

            def weighted(head, x_, v0_, v1_, w):
                if x_:
                    pe.wait_ge(pv_free, head)
                pe.matmul(pv[:, 0:2 * P], v0_, w[:, 0:2 * P], start=True, stop=False)
                pe.matmul(pv[:, P:2 * P], v1_, w[:, 2 * P:3 * P], start=False, stop=True)\
                  .then_inc(pv_full, 1)

            def mla_out(g, x_, v0, v1):
                pe.wait_ge(tp_free[(x_ + 1) % 2], (v1, v0)[x_ % 2] + (3, 4, 4, 5)[x_])
                weighted(GH * g + x_, x_, kvg[:, 0, x_, NOPE:], kvg[:, 1, x_, NOPE:], pt[:, x_ % 2, :])

            def mla_attention(g, j):
                v0, v1 = g * 5 + TP0["mla"], g * 4 + TP1["mla"]

                def q_k(x_):
                    turn((x_ + 1) % 2, (v1, v0)[x_ % 2] + (0, 1, 1, 2)[x_],
                         [qg[:, m, x_, 0:NOPE] for m in range(M)] + [kvg[:, m, x_, 0:NOPE] for m in range(M)])

                if j == 0:
                    pe.wait_ge(q_rope, g * 2 + 2)
                    for m in range(M):
                        pe.wait_ge(acc_free[0][m], g * 2 + ACC0["mla"] + 2)
                    turn(0, v0, [qrg[:, m, 2 * pr:2 * pr + 2, :].rearrange("p h c -> p (h c)")
                                 for pr in range(2) for m in range(M)])
                    q_k(0)
                elif j == 1:
                    q_k(1)
                    for m in range(M):
                        pe.wait_ge(acc_free[1][m], g * 2 + ACC1["mla"] + 2)
                    q_k(2)
                    mla_scores(g, 0, v0, v1)
                elif j == 2:
                    q_k(3)
                    mla_scores(g, 1, v0, v1)
                    mla_turn_p(g, 0, v0, v1)
                elif j == 3:
                    mla_scores(g, 2, v0, v1)
                    mla_turn_p(g, 1, v0, v1)
                    mla_out(g, 0, v0, v1)
                elif j == 4:
                    mla_scores(g, 3, v0, v1)
                    mla_turn_p(g, 2, v0, v1)
                    mla_out(g, 1, v0, v1)
                elif j == 5:
                    mla_turn_p(g, 3, v0, v1)
                    mla_out(g, 2, v0, v1)
                elif j == 6:
                    mla_out(g, 3, v0, v1)

            def mla_group(b, it, g, before):
                a0, a1 = g * 2 + ACC0["mla"], g * 2 + ACC1["mla"]
                for j in range(2):
                    products(b, it, j, 0, ct_hi, ct_lo, 2 * j, 2, CW, first=j == 0, last=j == 1,
                             free=a0 if j == 0 else None)
                    before(j)
                products(b, it, 2, 1, ct_hi, ct_lo, 0, KL, HQ - CW, first=True, last=True, free=a1)
                before(2)
                for j in range(3, 7):
                    a, k = (j - 3) // 2, (j - 3) % 2
                    if isinstance(g, int) and g == 0 and j == 3:
                        pe.wait_ge(tp_free[0], TP0["lat"] + 3)
                        pe.wait_ge(tp_free[1], TP1["lat"] + 2)
                    products(b, it, j, a, ct_hi, ct_lo, KL + 2 * k, 2, CW, first=k == 0, last=k == 1,
                             free=(a0 + 1, a1 + 1)[a] if k == 0 else None)
                    before(j)

            def project_out(b, phase, attention, heads0, nxt=None):
                for j in range(16):
                    c, k = WO[j]
                    if attention and c == 0:
                        pe.wait_ge(pv_free, heads0 + 2 * k + 2)
                    products(b, 0, j, c, ot_hi, ot_lo, 2 * k, 2, CW, first=k == 0, last=k == 7,
                             free=(ACC0, ACC1)[c][phase] + (0 if attention else 1) if k == 0 else None)
                    if attention:
                        attention(j)
                    elif j in (12, 13):
                        turn_h(nxt, j - 12)

            def gate_up(layer, b, it, c):
                gu, pr = f"gu{layer}", f"pair{layer}"
                for j in range(16):
                    products(b, it, j, j // 8, xt_hi, xt_lo, 2 * (j % 8), 2, CW, first=j % 8 == 0,
                             last=j % 8 == 7, free=c + (ACC0, ACC1)[j // 8][gu] if j % 8 == 0 else None)
                    if j == 1:
                        turn_pair(layer, c - 1, 0)
                    if j == 2:
                        turn_pair(layer, c - 1, 1)

            def turn_pair(layer, c, u):
                if u == 0:
                    for m in range(M):
                        pe.wait_ge(acc_free[1][m], c + (ACC1[f"gu{layer}"] + 1))
                turn(u, c + (TP0, TP1)[u][f"pair{layer}"], tiles_of(hm, 2 * u))

            def ffn(layer):
                first, loop = bodies[f"gu{layer}a"], bodies[f"gu{layer}"]
                gu = f"gu{layer}"
                first_chunk(gu, first, ACC0[gu])
                for j in range(8, 16):
                    products(first, 0, j, 1, xt_hi, xt_lo, 2 * (j % 8), 2, CW, first=j == 8, last=j == 15,
                             free=ACC1[gu] if j == 8 else None)
                with pe.Fori(0, PAIRS - 1) as it:
                    gate_up(layer, loop, it, it + 1)
                dn = f"down{layer}"
                for it, part in enumerate("ab"):
                    down = bodies[dn + part]
                    for j in range(44):
                        a, k = j // 22, j % 22
                        if down.name == "down1b" and j >= down.n - TAIL:
                            break
                        if k == 20 and j < 22 and part == "a":
                            pe.wait_ge(tp_free[0], TP0[f"pair{layer}"] + PAIRS)
                            pe.wait_ge(tp_free[1], TP1[f"pair{layer}"] + PAIRS)
                        products(down, 0, j, a, hid_hi, hid_lo, 2 * k, 2, CW, first=k == 0, last=k == 21,
                                 free=it + (ACC0, ACC1)[a][dn] if k == 0 else None)
                        if part == "a" and j in (1, 2):
                            turn_pair(layer, PAIRS - 1, j - 1)
                        if layer == 0 and part == "b" and j in (40, 41):
                            turn_h("sb", j - 40)

            def last_halves():
                b = bodies["down1b"]
                for m in range(M):
                    for j in range(b.n - TAIL, b.n):
                        used = (1, TAIL - 1)[m] if j == b.n - 1 else 0
                        products(b, 0, j, 1, hid_hi, hid_lo, 2 * (j - 22), 2, CW, last=j == b.n - 1,
                                 tokens=[m], used=used)

            def sb_attention(g, j):
                def head(x_):
                    return g * GH + x_
                if j == 0:
                    for m in range(M):
                        pe.wait_ge(acc_free[0][m], g * 2 + ACC0["sb"] + 2)
                        pe.wait_ge(acc_free[1][m], g + ACC1["sb"] + 1)
                if j < 4:
                    turn(0, g * GH + TP0["sba"] + j,
                         [s[:, m, j * P:(j + 1) * P] for s in (sq, sk) for m in range(M)])
                x_ = j - 1
                if 0 <= x_ < GH:
                    pe.wait_ge(tp_free[0], g * GH + TP0["sba"] + x_ + 1)
                    if x_ >= 2:
                        pe.wait_ge(a_exp_done, head(x_ - 1))
                    z = zb[x_ % 2]
                    pe.matmul(z[:, 0:2 * P], qkt[:, x_, 1, 0:P], qkt[:, x_, 0, :], start=True, stop=False,
                              skip_group_check=True)
                    pe.matmul(z[:, 2 * P:3 * P], qkt[:, x_, 1, P:2 * P], qkt[:, x_, 0, P:2 * P],
                              start=False, stop=False, skip_group_check=True).then_inc(z_full, 1)
                x_ = j - 3
                if 0 <= x_ < GH:
                    pe.wait_ge(a_done, head(x_) + 1)
                    weighted(g * GH + (HEADS + x_), x_, sv[:, 0, x_ * P:(x_ + 1) * P],
                             sv[:, 1, x_ * P:(x_ + 1) * P], pt[:, x_ % 2, :])
                x_ = j - 2
                if 0 <= x_ < GH:
                    pe.wait_ge(ssp_done, head(x_) + 1)
                    z, s_ = zb[x_ % 2], ssp[:, x_ % 2, :]
                    pe.matmul(z[:, 0:2 * P], neg_tri[:, :], s_[:, 0:2 * P], start=False, stop=False,
                              skip_group_check=True)
                    pe.matmul(z[:, P:2 * P], neg_one[:, :], s_[:, 2 * P:3 * P], start=False, stop=False,
                              skip_group_check=True)
                    pe.matmul(z[:, 2 * P:3 * P], neg_tri[:, :], s_[:, 2 * P:3 * P], start=False, stop=True,
                              skip_group_check=True).then_inc(logw_full, 1)

            def sb_group(b, it, g, attention):
                a0, a1 = g * 2 + ACC0["sb"], g + ACC1["sb"]
                for j in range(24):
                    c, k = SB[j]
                    products(b, it, j, c % 2, xt_hi, xt_lo, 2 * k, 2, CW, first=k == 0, last=k == 7,
                             free=(a0, a1, a0 + 1)[c] if k == 0 else None)
                    attention(j)

            pe.wait_ge(consts_done, CONSTS)
            turn_h("win", 0)
            pe.wait_ge(attn_gains_landed, 16)
            pe.transpose(sc[:, 0:2 * KD], gain_rows[0:2 * KD, :], ident[0:2 * KD, 0:2 * KD]).then_inc(gain_full, 1)
            turn_h("win", 1)
            b = bodies["win"]
            first_chunk("win", b, 0)
            for j in range(8, b.n):
                c, k = WIN[j]
                if j == KR_HALF:
                    for m in range(M):
                        pe.wait_ge(acc_free[0][m], 1)
                    pe.wait_ge(lo_done, st.number(b, 0, j) + 1)
                    o = acc[0][0][0:ROPE, 0:M * P]
                    for k in range(KD):
                        wh = w_hi[:, b.cut(j), k * ROPE:(k + 1) * ROPE]
                        wl = w_lo[:, b.cut(j), k * ROPE:(k + 1) * ROPE]
                        pe.matmul(o, wh, xt_hi[:, k, :], start=k == 0, stop=False)
                        pe.matmul(o, wh, xt_lo[:, k, :], start=False, stop=False)
                        mm = pe.matmul(o, wl, xt_hi[:, k, :], start=False, stop=k == KD - 1)
                    mm.then_inc(half_used, 1)
                else:
                    products(b, 0, j, c, xt_hi, xt_lo, 2 * k, 2, CW, first=k == 0, last=k == 7)
                if j == 8:
                    pe.wait_ge(small_landed, 16 * SMALL)
                    pe.wait_ge(gain_done, 1)
                    pe.transpose(sc[:, 0:NG], gain_rows[:, :], ident[0:NG, 0:NG]).then_inc(gain_full, 1)
                if j == 11:
                    for m in range(M):
                        pe.wait_ge(acc_free[0][m], 1)
                    turn(0, TP0["lat"], tiles_of(sg, 0))
                    turn(1, TP1["lat"], tiles_of(sg, 2))
                if j == 14:
                    for m in range(M):
                        pe.wait_ge(acc_free[0][m], 2)
                    pe.wait_ge(tp_free[0], TP0["lat"] + 1)
                    for m in range(M):
                        mm = pe.transpose(tp[0][:, m * ROPE:(m + 1) * ROPE], kr_turned[:, m * P:(m + 1) * P],
                                          ident[0:ROPE, 0:ROPE])
                    mm.then_inc(tp_full[0], 1)

            def latents_and_kr(j):
                if j == 0:
                    for m in range(M):
                        pe.wait_ge(acc_free[1][m], 1)
                    turn(0, TP0["lat"] + 2, tiles_of(hm, 0))
                    turn(1, TP1["lat"] + 1, tiles_of(hm, 2))
                if j == 1:
                    pe.wait_ge(kr_done, M * 2)
                    turn(0, TP0["lat"] + 3, [kr_pad[:, a, m, :] for a in range(2) for m in range(M)])

            pe.wait_ge(tp_free[0], TP0["lat"] + 1)
            pe.wait_ge(tp_free[1], TP1["lat"] + 1)
            mla_group(bodies["mla0"], 0, 0, latents_and_kr)
            with pe.Fori(0, GROUPS - 1) as it:
                mla_group(bodies["mla"], it, it + 1, lambda j: mla_attention(it, j))
            project_out(bodies["wo0a"], "wo0", lambda j: mla_attention(GROUPS - 1, j), 0)
            project_out(bodies["wo0b"], "wo0", None, 0, "gu0")
            ffn(0)

            b = bodies["sb0"]
            first_chunk("sb", b, ACC0["sb"])
            for j in range(8, 24):
                c, k = SB[j]
                products(b, 0, j, c % 2, xt_hi, xt_lo, 2 * k, 2, CW, first=k == 0, last=k == 7,
                         free=(0, ACC1["sb"], ACC0["sb"] + 1)[c] if k == 0 else None)
            with pe.Fori(0, GROUPS - 1) as it:
                sb_group(bodies["sb"], it, it + 1, lambda j: sb_attention(it, j))
            project_out(bodies["wo1a"], "wo1", lambda j: sb_attention(GROUPS - 1, j), HEADS)
            project_out(bodies["wo1b"], "wo1", None, HEADS, "gu1")
            ffn(1)
            last_halves()

        @block.scalar
        def _(act):
            def cut(target):
                if target is None:
                    return
                b, it, j = target
                act.wait_ge(landed[b.raw(j)], st.landed(b, it, j))
                if j in b.cut_gap:
                    act.wait_ge(half_used, st.number(b, it, j) - b.cut_gap[j])
                act.activation(w_hi[:, b.cut(j), :], w_raw[:, b.raw(j), :], ACT.Copy).then_inc(hi_done, 1)

            def run(name, side):
                b = bodies[name]
                if b.iters == 1:
                    for j in range(b.n):
                        cut(st.ahead(b, 0, j))
                        side(b, 0, j)
                else:
                    with act.Fori(0, b.iters) as it:
                        for j in range(b.n):
                            cut(st.ahead(b, it, j))
                            side(b, it, j)

            def chunk_full(b, it, j):
                act.wait_ge(half_used, st.number(b, it, j) + 1)

            def turned_hi(u, count, thi, dst, gains):
                act.wait_ge(tp_full[u], count)
                if gains is None:
                    act.activation(dst, tp[u][:, :].rearrange("p (t c) -> p t c", t=2), ACT.Copy)\
                       .then_inc(t_hi_done, 1)
                else:
                    act.activation(dst[:, 0, :], tp[u][:, 0:M * P], ACT.Copy, scale=gain[:, gains:gains + 1])
                    act.activation(dst[:, 1, :], tp[u][:, M * P:], ACT.Copy,
                                   scale=gain[:, gains + 1:gains + 2]).then_inc(t_hi_done, 1)

            def turned_h(phase, u, g0):
                turned_hi(u % 2, (TP0, TP1)[u % 2][phase] + u // 2 + 1, None,
                          xt_hi[:, 2 * u:2 * u + 2, :], g0 + 2 * u)

            def squares(src, scratch, halves=range(M)):
                for m in halves:
                    act.activation(scratch[m], src[:, m, :], ACT.Square, accum_out=ssq[:, m:m + 1])\
                       .then_inc(ssq_done, 1)

            def root(norm, c=slice(0, M)):
                act.wait_ge(ms_done, norm + 1)
                if norm:
                    act.wait_ge(rstd_done, norm)
                act.activation(ln_ms[:, c], ms[:, c], ACT.Ln).then_inc(ln_done, 1)
                act.wait_ge(ln_done, norm + 1)
                act.activation(y0[:, c], ln_ms[:, c], ACT.Exp, scale=-0.5).then_inc(y0_done, 1)

            def phase_start(phase, norm, g0, j):
                if j + 2 < 8:
                    turned_h(phase, j + 2, g0)
                if j in (5, 6):
                    if j == 5:
                        if phase == "win":
                            for c in range(D // CW):
                                act.wait_ge(x_landed[c], 16)
                        else:
                            for m in range(M):
                                act.wait_ge(acc_free[0][m], ACC0[phase])
                                act.wait_ge(acc_free[1][m], ACC1[phase])
                    squares(h, junk, [j - 5])
                if j == 7:
                    root(norm)

            act.dma_start(gain_rows[0:2 * KD, :], attn_norm.rearrange("l (k p) -> (l k) p", p=P))\
               .then_inc(attn_gains_landed, 16)
            act.dma_start(h[:, :, CW:2 * CW], x_v[:, :, CW:2 * CW]).then_inc(x_landed[1], 16)
            R2 = ROPE // 2
            act.preload_act_table_set("natural_log_exp_and_others")
            for j in range(LA):
                cut((bodies["win"], 0, j))
                if j == 0:
                    act.wait_ge(gain_done, 1)
                if j < 2:
                    turned_h("win", j, G_ATTN[0])

            small_junk = [pb[:, m, :].bitcast(BF16)[:, 0:LORA] for m in range(M)]

            def sines():
                act.wait_ge(angles_done, 1)
                act.activation(rope_s[:, :, R2:], red_s[:, :, :], ACT.Sin).then_inc(sin_done, 1)
                act.activation(rope_c[:, :, 0:R2], red_c[:, :, :], ACT.Sin).then_inc(sin_done, 1)
                act.activation(rope_c[:, :, R2:], red_c[:, :, :], ACT.Sin).then_inc(sin_done, 1)
                act.preload_act_table_set("natural_log_exp_and_others")

            def side_win(b, it, j):
                phase_start("win", N_ATTN0, G_ATTN[0], j)
                if j == 7:
                    chunk_full(b, it, j)
                    act.wait_ge(rstd_done, N_ATTN0 + 1)
                    act.activation(sg[:, 0, :], acc[0][0][:, :], ACT.Copy, scale=rstd[:, 0:1])\
                       .then_inc(acc_free[0][0], 1)
                if j == 8:
                    act.wait_ge(acc_free[0][0], 1)
                    act.wait_ge(acc_free[0][1], 1)
                    squares(sg, small_junk)
                if j == 9:
                    root(N_Q)
                if j == 11:
                    act.wait_ge(gain_done, 2)
                    turned_hi(0, TP0["lat"] + 1, None, ct_hi[:, 0:2, :], G_Q)
                    turned_hi(1, TP1["lat"] + 1, None, ct_hi[:, 2:4, :], G_Q + 2)
                if j == KR_HALF:
                    chunk_full(b, it, j)
                    act.activation(kr_turned[:, 0:P], acc[0][0][0:ROPE, 0:P], ACT.Copy)\
                       .then_inc(acc_free[0][0], 1)
                    sines()
                if j == 16:
                    chunk_full(b, it, j)
                    act.activation(hm[:, 0, :], acc[1][0][:, :], ACT.Copy, scale=rstd[:, 0:1])\
                       .then_inc(acc_free[1][0], 1)

            def mla_attention(g, j, take_q=lambda: None):
                v0, v1 = g * 5 + TP0["mla"], g * 4 + TP1["mla"]

                def q_k(x_):
                    act.wait_ge(tp_full[(x_ + 1) % 2], (v1, v0)[x_ % 2] + (1, 2, 2, 3)[x_])
                    act.activation(qkt[:, x_, :, :], tp[(x_ + 1) % 2][:, :].rearrange("p (s c) -> p s c", s=2),
                                   ACT.Copy).then_inc(tp_free[(x_ + 1) % 2], 1)

                def exps(x_):
                    act.wait_ge(max_done, g * GH + (x_ + 1))
                    a = x_ % 2
                    act.activation(pb[:, a, 0:P], sc[:, 0:P], ACT.Exp, bias=nmax_s[:, a, 0:1], scale=MLA_SCALE,
                                   accum_out=psums[:, a, 0:1])
                    act.activation(pb[:, a, P:3 * P], sc[:, P:3 * P], ACT.Exp, bias=nmax_s[:, a, 1:2],
                                   scale=MLA_SCALE, accum_out=psums[:, a, 1:2]).then_inc(exp_done, 1)

                if j == 0:
                    q_k(0)
                elif j == 1:
                    q_k(1)
                    q_k(2)
                    exps(0)
                elif j == 2:
                    q_k(3)
                    take_q()
                    exps(1)
                elif j == 3:
                    exps(2)
                elif j == 4:
                    exps(3)
                if 3 <= j <= 6:
                    out_hi(g * GH + (j - 3), ot_slot(g, j - 3))

            def ot_slot(g, x_):
                return bass.ds(g * GH + x_, 1)

            def out_hi(head, slot):
                act.wait_ge(pv_full, head + 1)
                act.activation(ot_hi[:, slot, :], pv[:, 0:M * P], ACT.Copy).then_inc(o_hi_done, 1)

            def mla_take(b, it, j, g):
                q_ = qg[:, 0, :, :].rearrange("p h c -> p (h c)")
                if j == (1 if b.name == "mla0" else 2):
                    chunk_full(b, it, j)
                    act.activation(q_[:, 0:CW], acc[0][0][:, :], ACT.Copy, scale=rstd_q[:, 0:1])\
                       .then_inc(acc_free[0][0], 1)
                if j == 2:
                    chunk_full(b, it, j)
                    act.activation(q_[:, CW:], acc[1][0][:, 0:256], ACT.Copy, scale=rstd_q[:, 0:1])\
                       .then_inc(acc_free[1][0], 1)
                if j in (4, 6):
                    a = (j - 4) // 2
                    chunk_full(b, it, j)
                    act.activation(kvg[:, 0, 2 * a:2 * a + 2, :].rearrange("p h c -> p (h c)"),
                                   acc[a][0][:, :], ACT.Copy, scale=rstd_kv[:, 0:1])\
                       .then_inc(acc_free[a][0], 1)

            def side_mla0(b, it, j):
                if j == 0:
                    turned_hi(0, TP0["lat"] + 3, None, ct_hi[:, 4:6, :], G_KV)
                    turned_hi(1, TP1["lat"] + 2, None, ct_hi[:, 6:8, :], G_KV + 2)
                    act.wait_ge(acc_free[1][0], 1)
                    act.wait_ge(acc_free[1][1], 1)
                    squares(hm, small_junk)
                if j == 1:
                    root(N_KV)
                    act.wait_ge(tp_full[0], TP0["lat"] + 4)
                    act.activation(krt[:, :, :], tp[0][:, :].rearrange("p (s c) -> p s c", s=2), ACT.Copy)\
                       .then_inc(tp_free[0], 1)
                    act.wait_ge(rstd_done, N_KV + 1)
                mla_take(b, it, j, 0)

            def side_mla(b, it, j):
                mla_attention(it, j, lambda: mla_take(b, it, 2, it + 1))
                if j != 2:
                    mla_take(b, it, j, it + 1)

            def side_wo0(b, it, j):
                mla_attention(GROUPS - 1, j)

            def first_turns(layer):
                def side(b, it, j):
                    if j in (12, 13):
                        turned_h(f"gu{layer}", j - 12, G_FFN[layer])
                return side

            def silu(layer, b, it, c):
                chunk_full(b, it, 7)
                for m in range(M):
                    act.wait_ge(acc_free[1][m], c + ACC1[f"gu{layer}"])
                    act.activation(sg[:, m, :], acc[0][m][:, :], ACT.Silu, scale=rstd[:, m:m + 1])\
                       .then_inc(acc_free[0][m], 1)

            def hidden_hi(layer, c, u):
                turned_hi(u, c + ((TP0, TP1)[u][f"pair{layer}"] + 1), None,
                          hid_hi[:, bass.ds(c * 4 + 2 * u, 2), :], None)

            def ffn(layer):
                norm = (N_FFN0, N_FFN1)[layer]
                gu = f"gu{layer}"

                def side_first(b, it, j):
                    phase_start(gu, norm, G_FFN[layer], j)
                    if j == 7:
                        act.wait_ge(rstd_done, norm + 1)
                        silu(layer, b, it, 0)

                def side_gu(b, it, j):
                    if j in (1, 2):
                        hidden_hi(layer, it, j - 1)
                    if j == 7:
                        silu(layer, b, it, it + 1)

                run(f"gu{layer}a", side_first)
                run(gu, side_gu)

            def last_pair(layer, j):
                if j in (1, 2):
                    hidden_hi(layer, PAIRS - 1, j - 1)

            def next_turns(b, it, j):
                if j in (40, 41):
                    turned_h("sb", j - 40, G_ATTN[1])

            def sb_attention(g, j):
                def head(x_):
                    return g * GH + x_
                if j < 4:
                    act.wait_ge(tp_full[0], g * GH + (TP0["sba"] + j + 1))
                    act.activation(qkt[:, j, :, :], tp[0][:, :].rearrange("p (s c) -> p s c", s=2), ACT.Copy)\
                       .then_inc(tp_free[0], 1)
                x_ = j - 1
                if 0 <= x_ < GH:
                    a, z = x_ % 2, zb[x_ % 2][:, 0:3 * P]
                    act.wait_ge(z_full, head(x_) + 1)
                    act.activation(sabs[:, a, :], z, ACT.Abs).then_inc(abs_done, 1)
                    act.wait_ge(abs_done, head(x_) + 1)
                    act.activation(sexp[:, a, :], sabs[:, a, :], ACT.Exp, scale=-1.0).then_inc(sexp_done, 1)
                    act.wait_ge(sexp_done, head(x_) + 1)
                    act.activation(sln[:, a, :], sexp[:, a, :], ACT.Ln, bias=1.0).then_inc(sln_done, 1)
                x_ = j - 3
                if 0 <= x_ < GH:
                    out_hi(head(x_) + HEADS, ot_slot(g, x_))
                x_ = j - 2
                if 0 <= x_ < GH:
                    act.wait_ge(logw_full, head(x_) + 1)
                    act.activation(pt[:, x_ % 2, :], zb[x_ % 2][:, 0:3 * P], ACT.Exp).then_inc(a_exp_done, 1)

            def sb_take(b, it, j):
                c, k = SB[j]
                if k == 7:
                    chunk_full(b, it, j)
                    act.activation((sq, sk, sv)[c][:, 0, :], acc[c % 2][0][:, :], ACT.Copy,
                                   scale=(rstd_q, rstd, rstd)[c][:, 0:1]).then_inc(acc_free[c % 2][0], 1)

            def side_sb0(b, it, j):
                phase_start("sb", N_ATTN1, G_ATTN[1], j)
                if j == 7:
                    act.wait_ge(rstd_done, N_ATTN1 + 1)
                    act.wait_ge(sb_scale_done, 1)
                sb_take(b, it, j)

            def side_sb(b, it, j):
                sb_attention(it, j)
                sb_take(b, it, j)

            run("win", side_win)
            run("mla0", side_mla0)
            run("mla", side_mla)
            run("wo0a", side_wo0)
            run("wo0b", first_turns(0))
            ffn(0)
            run("down0a", lambda b, it, j: last_pair(0, j))
            act.preload_act_table_set("natural_log_exp_and_others")
            run("down0b", next_turns)
            run("sb0", side_sb0)
            run("sb", side_sb)
            run("wo1a", lambda b, it, j: sb_attention(GROUPS - 1, j))
            run("wo1b", first_turns(1))
            ffn(1)

            def chunk_squares(n, m):
                c = slice(n * CW, (n + 1) * CW)
                act.wait_ge(acc_free[n % 2][m], (ACC0, ACC1)[n % 2]["down1"] + n // 2 + 1)
                act.activation(junk[m][:, c], h[:, m, c], ACT.Square, accum_out=ssq_part[:, m, n:n + 1])\
                   .then_inc(ssq_done, 1)

            def last_squares(n0):
                def side(b, it, j):
                    if n0 == 0:
                        last_pair(1, j)
                    if j % 22 == 21 and n0 + j // 22 < D // CW - 1:
                        for m in range(M):
                            chunk_squares(n0 + j // 22, m)
                return side

            run("down1a", last_squares(0))
            act.preload_act_table_set("natural_log_exp_and_others")
            run("down1b", last_squares(2))
            for m in range(M):
                chunk_squares(D // CW - 1, m)
                root(N_FINAL + m, slice(m, m + 1))
                act.wait_ge(rstd_done, N_FINAL + m + 1)
                act.wait_ge(gained, 3 * M)
                act.activation(h[:, m, 0:HW], h[:, m, 0:HW], ACT.Copy, scale=rstd[:, m:m + 1])\
                   .then_inc(out_act, 1)
                act.wait_ge(out_act, m + 1)
                act.dma_start(out_v[:, m, 0:HW], h[:, m, 0:HW]).then_inc(out_stored, 16)
            act.wait_ge(out_stored, 16 * 2 * M)

        @block.vector
        def _(dve):
            steps = [0]

            def chain(ins):
                steps[0] += 1
                ins.then_inc(dve_step, 1)
                dve.wait_ge(dve_step, steps[0])

            def cut(target):
                if target is None:
                    return
                b, it, j = target
                dve.wait_ge(hi_done, st.number(b, it, j) + 1)
                dve.tensor_tensor(w_lo[:, b.cut(j), :], w_raw[:, b.raw(j), :], w_hi[:, b.cut(j), :].bitcast(F32),
                                  ALU.subtract).then_inc(lo_done, 1)

            def run(name, side, urgent=lambda b, it, j: None):
                b = bodies[name]
                if b.iters == 1:
                    for j in range(b.n):
                        urgent(b, 0, j)
                        cut(st.ahead(b, 0, j))
                        side(b, 0, j)
                else:
                    with dve.Fori(0, b.iters) as it:
                        for j in range(b.n):
                            urgent(b, it, j)
                            cut(st.ahead(b, it, j))
                            side(b, it, j)

            def chunk_full(b, it, j):
                dve.wait_ge(half_used, st.number(b, it, j) + 1)

            def turned_lo(u, count, lo, hi, gains):
                dve.wait_ge(t_hi_done, count)
                if gains is None:
                    dve.tensor_tensor(lo, tp[u][:, :].rearrange("p (t c) -> p t c", t=2), hi.bitcast(F32),
                                      ALU.subtract).then_inc(tp_free[u], 1)
                else:
                    for n in range(2):
                        ins = dve.scalar_tensor_tensor(
                            out=lo[:, n, :], in0=tp[u][:, n * M * P:(n + 1) * M * P],
                            scalar=gain[:, gains + n:gains + n + 1], in1=hi[:, n, :].bitcast(F32),
                            op0=ALU.mult, op1=ALU.subtract)
                    ins.then_inc(tp_free[u], 1)

            def turned_h(phase, u, g0):
                turned_lo(u % 2, THI[phase] + u + 1, xt_lo[:, 2 * u:2 * u + 2, :], xt_hi[:, 2 * u:2 * u + 2, :],
                          g0 + 2 * u)

            def mean_square(norm, width):
                dve.wait_ge(ssq_done, M * (norm + 1))
                dve.tensor_scalar(ms[:, :], ssq[:, :], 1.0 / width, EPS, ALU.mult, ALU.add).then_inc(ms_done, 1)

            def refine(norm, out_, c=slice(0, M)):
                dve.wait_ge(y0_done, norm + 1)
                if norm:
                    dve.wait_ge(rstd_done, norm)
                chain(dve.tensor_tensor(nt[:, c], y0[:, c], y0[:, c], ALU.mult))
                chain(dve.tensor_tensor(nt[:, c], nt[:, c], ms[:, c], ALU.mult))
                chain(dve.tensor_scalar(nt[:, c], nt[:, c], -0.5, 1.5, ALU.mult, ALU.add))
                dve.tensor_tensor(out_[:, c], y0[:, c], nt[:, c], ALU.mult).then_inc(rstd_done, 1)

            def phase_start(phase, norm, g0, j):
                if j + 2 < 8:
                    turned_h(phase, j + 2, g0)
                if j == 6:
                    mean_square(norm, D)
                if j == 7:
                    refine(norm, rstd)

            dve.wait_ge(gain_full, 1)
            dve.tensor_copy(gain[:, 0:2 * KD], sc[:, 0:2 * KD]).then_inc(gain_done, 1)
            for j in range(LA):
                cut((bodies["win"], 0, j))
                if j == 0:
                    dve.wait_ge(gain_done, 1)
                if j < 2:
                    turned_h("win", j, G_ATTN[0])

            R2 = ROPE // 2

            def reduce_angles():
                TWO_PI = 2.0 * np.pi
                C1 = 6.28125
                C2 = float(np.float32(np.round((TWO_PI - C1) * 2.0 ** 21) / 2.0 ** 21))
                C3 = TWO_PI - C1 - C2
                ROUND = 1.5 * 2.0 ** 23
                PI_LESS = 3.1415925
                dve.wait_ge(pos_landed, 32)
                chain(dve.tensor_copy(pos_f[:, :], pos_i[:, :]))
                for m in range(M):
                    ins = dve.tensor_scalar(ang[:, m, :], inv_f[:, :], pos_f[:, m:m + 1], None, ALU.mult)
                chain(ins)
                chain(dve.tensor_scalar(turns[:, :, :], ang[:, :, :], 1.0 / TWO_PI, ROUND, ALU.mult, ALU.add))
                chain(dve.tensor_scalar(turns[:, :, :], turns[:, :, :], ROUND, None, ALU.subtract))
                for c in (C1, C2, C3):
                    chain(dve.scalar_tensor_tensor(out=ang[:, :, :], in0=turns[:, :, :], scalar=-c, in1=ang[:, :, :],
                                                   op0=ALU.mult, op1=ALU.add))
                chain(dve.tensor_scalar(red_c[:, :, :], ang[:, :, :], np.pi / 2, None, ALU.add))
                chain(dve.tensor_scalar(turns[:, :, :], red_c[:, :, :], np.pi, -TWO_PI, ALU.is_gt, ALU.mult))
                chain(dve.tensor_tensor(red_c[:, :, :], red_c[:, :, :], turns[:, :, :], ALU.add))
                chain(dve.tensor_scalar(red_c[:, :, :], red_c[:, :, :], PI_LESS, -PI_LESS, ALU.min, ALU.max))
                dve.tensor_scalar(red_s[:, :, :], ang[:, :, :], PI_LESS, -PI_LESS, ALU.min, ALU.max)\
                   .then_inc(angles_done, 1)

            def turn_by_angles(x_, m, heads, step_sem, before, outs, done):
                cos = rope_c[:, m, :].unsqueeze(1).broadcast_to([P, heads, ROPE])
                sin = rope_s[:, m, :].unsqueeze(1).broadcast_to([P, heads, ROPE])
                t1, t2 = r_t1[:, m, 0:heads, :], r_t2[:, m, 0:heads, :]
                dve.tensor_tensor(t1, x_, cos, ALU.mult).then_inc(step_sem, 1)
                dve.tensor_tensor(t2[:, :, 0:R2], x_[:, :, R2:], sin[:, :, 0:R2], ALU.mult).then_inc(step_sem, 1)
                dve.tensor_tensor(t2[:, :, R2:], x_[:, :, 0:R2], sin[:, :, R2:], ALU.mult).then_inc(step_sem, 1)
                dve.wait_ge(step_sem, before + 3)
                for o in outs:
                    dve.tensor_tensor(o, t1, t2, ALU.add).then_inc(done, 1)

            def side_win(b, it, j):
                phase_start("win", N_ATTN0, G_ATTN[0], j)
                if j == 7:
                    chunk_full(b, it, j)
                    dve.wait_ge(rstd_done, N_ATTN0 + 1)
                    dve.tensor_scalar(sg[:, 1, :], acc[0][1][:, :], rstd[:, 1:2], None, ALU.mult)\
                       .then_inc(acc_free[0][1], 1)
                if j == 8:
                    mean_square(N_Q, LORA)
                if j == 8:
                    dve.wait_ge(gain_full, 2)
                    dve.tensor_copy(gain[:, 2 * KD:], sc[:, 2 * KD:NG]).then_inc(gain_done, 1)
                if j == 13:
                    dve.wait_ge(sin_done, 3)
                    dve.tensor_scalar(rope_s[:, :, 0:R2], rope_s[:, :, R2:], -1.0, None, ALU.mult)\
                       .then_inc(rope_ready, 1)
                if j == 9:
                    refine(N_Q, rstd_q)
                    reduce_angles()
                if j == 11:
                    dve.wait_ge(gain_done, 2)
                    turned_lo(0, THI["lat"] + 1, ct_lo[:, 0:2, :], ct_hi[:, 0:2, :], G_Q)
                    turned_lo(1, THI["lat"] + 2, ct_lo[:, 2:4, :], ct_hi[:, 2:4, :], G_Q + 2)
                if j == KR_HALF:
                    dve.wait_ge(acc_free[0][0], 2)
                    dve.tensor_copy(kr_turned[:, P:], acc[0][0][0:ROPE, P:M * P]).then_inc(acc_free[0][1], 1)
                if j == 14:
                    dve.wait_ge(tp_full[0], TP0["lat"] + 2)
                    for m in range(M):
                        ins = dve.tensor_scalar(kr[:, m, :], tp[0][:, m * ROPE:(m + 1) * ROPE], rstd[:, m:m + 1],
                                                None, ALU.mult)
                    ins.then_inc(tp_free[0], 1)
                    dve.wait_ge(rope_ready, 1)
                    dve.wait_ge(tp_free[0], TP0["lat"] + 2)
                    for m in range(M):
                        turn_by_angles(kr[:, m:m + 1, :], m, 1, kr_step, 3 * m,
                                       [kr_pad[:, 0, m:m + 1, 0:ROPE], kr_pad[:, 1, m:m + 1, ROPE:]], kr_done)
                if j == 16:
                    chunk_full(b, it, j)
                    dve.tensor_scalar(hm[:, 1, :], acc[1][1][:, :], rstd[:, 1:2], None, ALU.mult)\
                       .then_inc(acc_free[1][1], 1)

            def out_lo(head, slot):
                dve.wait_ge(o_hi_done, head + 1)
                dve.tensor_tensor(ot_lo[:, slot, :], pv[:, 0:M * P], ot_hi[:, slot, :].bitcast(F32),
                                  ALU.subtract).then_inc(pv_free, 1)

            def maxima(g, j):
                x_ = j - 1
                a = x_ % 2
                dve.wait_ge(sc_full, g * GH + (x_ + 1))
                dve.tensor_reduce(nmax[:, a, 0:1], sc[:, 0:P], AX_X, ALU.max).then_inc(nmax_done, 1)
                dve.tensor_reduce(nmax[:, a, 1:2], sc[:, P:3 * P], AX_X, ALU.max).then_inc(nmax_done, 1)
                dve.wait_ge(nmax_done, g * (2 * GH) + 2 * (x_ + 1))
                dve.tensor_scalar(nmax_s[:, a, :], nmax[:, a, :], -MLA_SCALE, None, ALU.mult)\
                   .then_inc(max_done, 1)

            def mla_attention(g, j):
                v0, v1 = g * 5 + TP0["mla"], g * 4 + TP1["mla"]

                def head(x_):
                    return g * GH + x_

                def normalise(x_):
                    a = x_ % 2
                    dve.wait_ge(exp_done, head(x_) + 1)
                    dve.reciprocal(prec[:, a, :], psums[:, a, :]).then_inc(prec_done, 1)
                    dve.wait_ge(prec_done, head(x_) + 1)
                    dve.tensor_scalar(pb[:, a, 0:P], pb[:, a, 0:P], prec[:, a, 0:1], None, ALU.mult)
                    dve.tensor_scalar(pb[:, a, P:3 * P], pb[:, a, P:3 * P], prec[:, a, 1:2], None, ALU.mult)\
                       .then_inc(p_done, 1)

                def take_p(x_):
                    dve.wait_ge(tp_full[(x_ + 1) % 2], (v1, v0)[x_ % 2] + (3, 4, 4, 5)[x_])
                    dve.tensor_copy(pt[:, x_ % 2, :], tp[(x_ + 1) % 2][:, 0:3 * P])\
                       .then_inc(tp_free[(x_ + 1) % 2], 1)

                if j == 0:
                    dve.wait_ge(tp_full[0], v0 + 1)
                    dve.tensor_copy(qrt[:, :, :], tp[0][:, :].rearrange("p (s c) -> p s c", s=2))\
                       .then_inc(tp_free[0], 1)
                if 1 <= j < GH:
                    maxima(g, j)
                if j == 1:
                    normalise(0)
                elif j == 2:
                    take_p(0)
                    normalise(1)
                elif j == 3:
                    take_p(1)
                    out_lo(head(0), bass.ds(head(0), 1))
                    normalise(2)
                elif j == 4:
                    take_p(2)
                    out_lo(head(1), bass.ds(head(1), 1))
                    normalise(3)
                elif j == 5:
                    take_p(3)
                    out_lo(head(2), bass.ds(head(2), 1))
                elif j == 6:
                    out_lo(head(3), bass.ds(head(3), 1))

            def mla_take(b, it, j, g):
                q_ = qg[:, 1, :, :].rearrange("p h c -> p (h c)")
                if j == (1 if b.name == "mla0" else 2):
                    chunk_full(b, it, j)
                    dve.tensor_scalar(q_[:, 0:CW], acc[0][1][:, :], rstd_q[:, 1:2], None, ALU.mult)\
                       .then_inc(acc_free[0][1], 1)
                if j == 2:
                    chunk_full(b, it, j)
                    dve.tensor_scalar(q_[:, CW:], acc[1][1][:, 0:256], rstd_q[:, 1:2], None, ALU.mult)\
                       .then_inc(acc_free[1][1], 1)
                if j == 5:
                    for m in range(M):
                        dve.wait_ge(acc_free[0][m], g * 2 + ACC0["mla"] + 1)
                        dve.wait_ge(acc_free[1][m], g * 2 + ACC1["mla"] + 1)
                        qr = qg[:, m, :, NOPE:NOPE + ROPE]
                        turn_by_angles(qr, m, GH, q_step, g * 6 + 3 * m, [qrg[:, m, :, :]], q_rope)
                if j in (4, 6):
                    a = (j - 4) // 2
                    chunk_full(b, it, j)
                    dve.tensor_scalar(kvg[:, 1, 2 * a:2 * a + 2, :].rearrange("p h c -> p (h c)"),
                                      acc[a][1][:, :], rstd_kv[:, 1:2], None, ALU.mult)\
                       .then_inc(acc_free[a][1], 1)

            def side_mla0(b, it, j):
                if j == 0:
                    turned_lo(0, THI["lat"] + 3, ct_lo[:, 4:6, :], ct_hi[:, 4:6, :], G_KV)
                    turned_lo(1, THI["lat"] + 4, ct_lo[:, 6:8, :], ct_hi[:, 6:8, :], G_KV + 2)
                    mean_square(N_KV, LORA)
                if j == 1:
                    refine(N_KV, rstd_kv)
                    dve.wait_ge(rstd_done, N_KV + 1)
                mla_take(b, it, j, 0)

            def side_mla(b, it, j):
                if j == 2:
                    dve.wait_ge(tp_full[0], it * 5 + (TP0["mla"] + 3))
                    mla_take(b, it, j, it + 1)
                mla_attention(it, j)
                if j != 2:
                    mla_take(b, it, j, it + 1)

            def add_chunk(b, it, j, a, n):
                chunk_full(b, it, j)
                cols = bass.ds(n * CW, CW)
                for m in range(M):
                    dve.tensor_tensor(h[:, m, cols], acc[a][m][:, :], h[:, m, cols], ALU.add)\
                       .then_inc(acc_free[a][m], 1)

            def wo_adds(n, layer=None):
                def adds(b, it, j):
                    c, k = WO[j]
                    if k == 7:
                        add_chunk(b, it, j, c, n + c)
                    if layer is not None and j in (12, 13):
                        turned_h(f"gu{layer}", j - 12, G_FFN[layer])
                return adds

            def down_adds(n, layer):
                def adds(b, it, j):
                    if n == 0 and j in (1, 2):
                        hidden_lo(layer, PAIRS - 1, j - 1)
                    if layer == 0 and n == 2 and j in (40, 41):
                        turned_h("sb", j - 40, G_ATTN[1])
                    if j % 22 == 21 and not (b.name == "down1b" and j == 43):
                        add_chunk(b, it, j, j // 22, n + j // 22)
                return adds

            def times_up(layer, b, it, c):
                chunk_full(b, it, 15)
                for m in range(M):
                    dve.wait_ge(acc_free[0][m], c + (ACC0[f"gu{layer}"] + 1))
                    dve.scalar_tensor_tensor(out=hm[:, m, :], in0=acc[1][m][:, :], scalar=rstd[:, m:m + 1],
                                             in1=sg[:, m, :], op0=ALU.mult, op1=ALU.mult)\
                       .then_inc(acc_free[1][m], 1)

            def hidden_lo(layer, c, u):
                k = bass.ds(c * 4 + 2 * u, 2)
                turned_lo(u, c * 2 + (THI[f"pair{layer}"] + u + 1), hid_lo[:, k, :], hid_hi[:, k, :], None)

            def ffn(layer):
                norm = (N_FFN0, N_FFN1)[layer]
                gu = f"gu{layer}"

                def side_first(b, it, j):
                    phase_start(gu, norm, G_FFN[layer], j)
                    if j == 15:
                        dve.wait_ge(rstd_done, norm + 1)
                        times_up(layer, b, it, 0)

                def side_gu(b, it, j):
                    if j in (1, 2):
                        hidden_lo(layer, it, j - 1)
                    if j == 15:
                        times_up(layer, b, it, it + 1)

                run(f"gu{layer}a", side_first)
                run(gu, side_gu)

            def sb_attention(g, j):
                def head(x_):
                    return g * GH + x_

                def diagonal(t_):
                    return t_.rearrange("p (n c) -> p n c", n=3)[:, 0:3:2, :]

                keep = strict[:, :].unsqueeze(1).broadcast_to([P, 2, P])
                x_ = j - 1
                if 0 <= x_ < GH:
                    a = x_ % 2
                    dve.wait_ge(sln_done, head(x_) + 1)
                    dve.scalar_tensor_tensor(out=ssp[:, a, :], in0=zb[a][:, 0:3 * P], scalar=0.0,
                                             in1=sln[:, a, :], op0=ALU.max, op1=ALU.add).then_inc(ssp_step, 1)
                    dve.wait_ge(ssp_step, head(x_) + 1)
                    s_ = diagonal(ssp[:, a, :])
                    dve.tensor_tensor(s_, s_, keep, ALU.mult).then_inc(ssp_done, 1)
                x_ = j - 3
                if 0 <= x_ < GH:
                    out_lo(head(x_) + HEADS, bass.ds(head(x_), 1))
                x_ = j - 2
                if 0 <= x_ < GH:
                    dve.wait_ge(a_exp_done, head(x_) + 1)
                    w_ = diagonal(pt[:, x_ % 2, :])
                    dve.scalar_tensor_tensor(out=w_, in0=w_, scalar=BIG, in1=keep, op0=ALU.min, op1=ALU.mult)\
                       .then_inc(a_done, 1)

            def sb_take(b, it, j):
                c, k = SB[j]
                if k == 7:
                    chunk_full(b, it, j)
                    dve.tensor_scalar((sq, sk, sv)[c][:, 1, :], acc[c % 2][1][:, :],
                                      (rstd_q, rstd, rstd)[c][:, 1:2], None, ALU.mult)\
                       .then_inc(acc_free[c % 2][1], 1)

            def side_sb0(b, it, j):
                phase_start("sb", N_ATTN1, G_ATTN[1], j)
                if j == 7:
                    dve.wait_ge(rstd_done, N_ATTN1 + 1)
                    dve.tensor_scalar(rstd_q[:, :], rstd[:, :], SB_SCALE, None, ALU.mult)\
                       .then_inc(sb_scale_done, 1)
                    dve.wait_ge(sb_scale_done, 1)
                sb_take(b, it, j)

            def side_sb(b, it, j):
                sb_attention(it, j)
                sb_take(b, it, j)

            run("win", side_win)
            run("mla0", side_mla0)
            run("mla", side_mla, lambda b, it, j: maxima(it, j) if j == GH else None)

            def side_wo0(b, it, j):
                mla_attention(GROUPS - 1, j)
                wo_adds(0)(b, it, j)

            def side_wo1(b, it, j):
                sb_attention(GROUPS - 1, j)
                wo_adds(0)(b, it, j)

            run("wo0a", side_wo0, lambda b, it, j: maxima(GROUPS - 1, j) if j == GH else None)
            run("wo0b", wo_adds(2, 0))
            ffn(0)
            run("down0a", down_adds(0, 0))
            run("down0b", down_adds(2, 0))
            run("sb0", side_sb0)
            run("sb", side_sb)
            run("wo1a", side_wo1)
            run("wo1b", wo_adds(2, 1))
            ffn(1)
            run("down1a", down_adds(0, 1))

            def side_last(b, it, j):
                if j in (1, 2, 25):
                    n = {1: 0, 2: 1, 25: 2}[j]
                    dve.wait_ge(gfin_landed, 16)
                    dve.wait_ge(ssq_done, M * N_FINAL + M * (n + 1))
                    c = slice(n * CW, (n + 1) * CW)
                    for m in range(M):
                        dve.tensor_tensor(h[:, m, c], h[:, m, c], gfin[:, c], ALU.mult).then_inc(gained, 1)
                down_adds(2, 1)(b, it, j)

            run("down1b", side_last)
            b, last = bodies["down1b"], slice(D - CW, D)
            for m in range(M):
                dve.wait_ge(half_used, st.number(b, 0, b.n - TAIL) + (1, TAIL)[m])
                dve.tensor_tensor(h[:, m, last], acc[1][m][:, :], h[:, m, last], ALU.add)\
                   .then_inc(acc_free[1][m], 1)
                dve.wait_ge(ssq_done, M * N_FINAL + M * (D // CW - 1) + m + 1)
                chain(dve.tensor_reduce(ssq[:, m:m + 1], ssq_part[:, m, :], AX_X, ALU.add))
                dve.tensor_scalar(ms[:, m:m + 1], ssq[:, m:m + 1], 1.0 / D, EPS, ALU.mult, ALU.add)\
                   .then_inc(ms_done, 1)
                refine(N_FINAL + m, rstd, slice(m, m + 1))
                dve.wait_ge(rstd_done, N_FINAL + m + 1)
                dve.wait_ge(gained, 3 * M)
                dve.tensor_scalar(h[:, m, HW:D - CW], h[:, m, HW:D - CW], rstd[:, m:m + 1], None, ALU.mult)
                dve.scalar_tensor_tensor(out=h[:, m, last], in0=h[:, m, last], scalar=rstd[:, m:m + 1],
                                         in1=gfin[:, last], op0=ALU.mult, op1=ALU.mult).then_inc(out_dve, 1)


_INS = ["x", "positions", "attn_norm", "mla_w_in", "mla_q_norm", "mla_kv_norm", "mla_w_uq", "mla_w_ukv",
        "mla_w_o", "sb_w_in", "sb_w_o", "ffn_norm", "ffn_w_gate_up", "ffn_w_down", "final_norm"]


def kernel(**inputs):
    import concourse.bacc as _bacc
    from concourse.bass_utils import run_bass_kernel_spmd as _run

    nc = _bacc.Bacc("TRN2", target_bir_lowering=False, num_devices=1, dynamic_dma_scratch_size=1024)
    arrays, args = {}, []
    values = {name: np.ascontiguousarray(inputs[name]) for name in _INS}
    values["inv_freq"] = (np.float32(THETA) ** (-np.arange(0, ROPE, 2, dtype=np.float32) / np.float32(ROPE)))
    for name, a in values.items():
        arrays[f"in_{name}_dram"] = a
        args.append(nc.dram_tensor(f"in_{name}_dram", a.shape, mybir.dt.from_np(a.dtype), kind="ExternalInput").ap())
    out = nc.dram_tensor("out_0_dram", (1, M * P, D), F32, kind="ExternalOutput").ap()
    trunk(nc, *args, out)
    r = _run(nc, [arrays], core_ids=[0])
    return r.results[0]["out_0_dram"]
```
